# Optimizing a Trainium2 kernel written in Bass

```python
import math
import jax, jax.numpy as jnp
from jax import lax
import numpy as np

D_MODEL = 1024
BATCH = 1
SEQ = 256
DEPTH = 2

CTX_LEN = 256
GRID_W = 64
N_MOD = 9
EPS = 1e-6
D_FF = 256 * (-(-(8 * D_MODEL // 3) // 256))

SSD_HEAD_DIM = 64
SSD_HEADS = D_MODEL // SSD_HEAD_DIM
SSD_INNER = SSD_HEADS * SSD_HEAD_DIM
SSD_GROUPS = 2
SSD_STATE = 128
SSD_CONV = 5
SSD_CHUNK = 128
CONV_DIM = SSD_INNER + 2 * SSD_GROUPS * SSD_STATE

POOL_WINDOWS = (2, 4, 8, 16)
N_POOL = len(POOL_WINDOWS)
POOL_WIDTH = D_MODEL
POOL_GROUP = POOL_WIDTH // N_POOL

MIX_A_WIDTH = SSD_INNER + POOL_WIDTH
IN_A = SSD_INNER + CONV_DIM + 2 * SSD_HEADS + POOL_WIDTH

NA_HEAD_DIM = 64
NA_HEADS = D_MODEL // NA_HEAD_DIM
NA_WIDTH = NA_HEADS * NA_HEAD_DIM
WIN_ROWS = 8
WIN_COLS = 16
COL_BLOCK = 16
COL_BAND = COL_BLOCK + WIN_COLS

N_EVEN = (DEPTH + 1) // 2
N_ODD = DEPTH // 2

kernel_name = 'hybrid_ssd_pool_natten_macaron_dit'

def _rmsnorm(h, g):
    hf = h.astype(jnp.float32)
    y = hf * lax.rsqrt(jnp.mean(hf * hf, axis=-1, keepdims=True) + EPS) * g.astype(jnp.float32)
    return y.astype(h.dtype)

def _modnorm(h, g, shift, scale):
    return _rmsnorm(h, g) * (1 + scale) + shift

def _swiglu(h, w1, w3, w2):
    return (jax.nn.silu(h @ w1) * (h @ w3)) @ w2

def _dwconv(u, w, b):
    ch = u.shape[-1]
    out = lax.conv_general_dilated(
        u, w[:, None, :].astype(u.dtype), window_strides=(1,),
        padding=[(SSD_CONV // 2, SSD_CONV // 2)],
        dimension_numbers=('NWC', 'WIO', 'NWC'), feature_group_count=ch)
    return out + b

def _ssd_chunked(xs, dt, a_coef, bm, cm, h0):
    bsz, l, nh, hp = xs.shape
    g = bm.shape[2]
    r = nh // g
    nc = l // SSD_CHUNK
    xc = (xs * dt[..., None]).reshape(bsz, nc, SSD_CHUNK, g, r, hp)
    bc = bm.reshape(bsz, nc, SSD_CHUNK, g, -1)
    cc = cm.reshape(bsz, nc, SSD_CHUNK, g, -1)
    acum = jnp.cumsum((dt * a_coef).reshape(bsz, nc, SSD_CHUNK, g, r), axis=2)
    at = jnp.moveaxis(acum, 2, -1)
    lower = jnp.tril(jnp.ones((SSD_CHUNK, SSD_CHUNK), dtype=bool))
    seg = jnp.exp(jnp.where(lower, at[..., :, None] - at[..., None, :], -jnp.inf))
    cb = jnp.einsum('bclgn,bcsgn->bcgls', cc, bc)
    y_diag = jnp.einsum('bcgls,bcgrls,bcsgrp->bclgrp', cb, seg, xc)
    decay_to_end = jnp.exp(acum[:, :, -1:] - acum)
    states = jnp.einsum('bclgn,bclgr,bclgrp->bcgrpn', bc, decay_to_end, xc)
    chunk_decay = jnp.exp(acum[:, :, -1])

    def step(h, inp):
        s_c, d_c = inp
        return h * d_c[..., None, None] + s_c, h

    h_last, h_prev = lax.scan(step, h0, (jnp.moveaxis(states, 1, 0), jnp.moveaxis(chunk_decay, 1, 0)))
    h_prev = jnp.moveaxis(h_prev, 0, 1)
    y_off = jnp.einsum('bclgn,bcgrpn,bclgr->bclgrp', cc, h_prev, jnp.exp(acum))
    return (y_diag + y_off).reshape(bsz, l, nh, hp), h_last

def _multiscale_pool(up, pool_w, pool_scale):
    bsz, l, _ = up.shape
    u = up.astype(jnp.float32).reshape(bsz, l, N_POOL, POOL_GROUP)
    cs = jnp.concatenate([jnp.zeros((bsz, 1, N_POOL, POOL_GROUP), jnp.float32), jnp.cumsum(u, axis=1)], axis=1)
    t = np.arange(l)[:, None]
    w = np.array(POOL_WINDOWS)[None, :]
    lo = np.clip(t - w // 2, 0, l - 1)
    hi = np.clip(t + w - 1 - w // 2, 0, l - 1)
    gi = np.arange(N_POOL)[None, :]
    win_sum = cs[:, hi + 1, gi] - cs[:, lo, gi]
    mean = win_sum / (hi - lo + 1).astype(np.float32)[None, :, :, None]
    mixed = jnp.einsum('blgc,gcd->blgd', mean - u, pool_w.astype(jnp.float32))
    return (mixed.reshape(bsz, l, POOL_WIDTH) * pool_scale.astype(jnp.float32)).astype(up.dtype)

def _ssd_pool_mixer(hl, hc, in_w, conv_w, conv_b, dt_bias, a_log, d_skip, gn_g, pool_w, pool_scale, out_w, need_ctx_out):
    f32 = jnp.float32
    a_coef = -jnp.exp(a_log.astype(f32))
    dt_b = dt_bias.astype(f32)
    d_h = d_skip.astype(f32)[:, None]
    splits = [SSD_INNER, SSD_INNER + CONV_DIM, SSD_INNER + CONV_DIM + 2 * SSD_HEADS]

    def project(h):
        bsz, l, _ = h.shape
        z, xbc, dt_raw, up = jnp.split(h @ in_w, splits, axis=-1)
        xbc = jax.nn.silu(_dwconv(xbc, conv_w, conv_b)).astype(f32)
        xs, bm, cm = jnp.split(xbc, [SSD_INNER, SSD_INNER + SSD_GROUPS * SSD_STATE], axis=-1)
        xs = xs.reshape(bsz, l, SSD_HEADS, SSD_HEAD_DIM)
        bm = bm.reshape(bsz, l, SSD_GROUPS, SSD_STATE)
        cm = cm.reshape(bsz, l, SSD_GROUPS, SSD_STATE)
        dt = jax.nn.softplus(dt_raw.astype(f32).reshape(bsz, l, 2, SSD_HEADS) + dt_b)
        return z, xs, bm, cm, dt, up

    def scan(seq, direction, h0):
        _, xs, bm, cm, dt, _ = seq
        if direction == 1:
            flip = lambda a: jnp.flip(a, axis=1)
        else:
            flip = lambda a: a
        y, h_last = _ssd_chunked(flip(xs), flip(dt[:, :, direction]), a_coef[direction], flip(bm), flip(cm), h0)
        return flip(y), h_last

    def finish(h, seq, y_f, y_b):
        z, xs, _, _, _, up = seq
        bsz, l, _ = h.shape
        y = (y_f + y_b + d_h * xs).reshape(bsz, l, SSD_INNER) * jax.nn.silu(z.astype(f32))
        y = _rmsnorm(y, gn_g).astype(h.dtype)
        pooled = _multiscale_pool(up, pool_w, pool_scale)
        return jnp.concatenate([y, pooled], axis=-1) @ out_w

    seq_c = project(hc)
    seq_l = project(hl)
    h0 = jnp.zeros((hc.shape[0], SSD_GROUPS, SSD_HEADS // SSD_GROUPS, SSD_HEAD_DIM, SSD_STATE), f32)
    yc_f, hc_f = scan(seq_c, 0, h0)
    yc_b, hc_b = scan(seq_c, 1, h0)
    yl_f, _ = scan(seq_l, 0, hc_f)
    yl_b, _ = scan(seq_l, 1, hc_b)
    out_l = finish(hl, seq_l, yl_f, yl_b)
    out_c = finish(hc, seq_c, yc_f, yc_b) if need_ctx_out else None
    return out_l, out_c

def _na_mixer(hl, hc, qkv_w, rpb, out_w, need_ctx_out):
    f32 = jnp.float32
    bsz, l, _ = hl.shape
    rows = l // GRID_W
    kr = min(WIN_ROWS, rows)
    qscale = NA_HEAD_DIM ** -0.5

    t = (hl @ qkv_w).reshape(bsz, l, 3, NA_HEADS, NA_HEAD_DIM)
    q = (t[:, :, 0] * qscale).reshape(bsz, rows, GRID_W, NA_HEADS, NA_HEAD_DIM)
    k = t[:, :, 1].reshape(bsz, rows, GRID_W, NA_HEADS, NA_HEAD_DIM)
    v = t[:, :, 2].reshape(bsz, rows, GRID_W, NA_HEADS, NA_HEAD_DIM)
    if need_ctx_out:
        tc = (hc @ qkv_w).reshape(hc.shape[0], hc.shape[1], 3, NA_HEADS, NA_HEAD_DIM)
    else:
        tc = (hc @ qkv_w[:, NA_WIDTH:]).reshape(hc.shape[0], hc.shape[1], 2, NA_HEADS, NA_HEAD_DIM)
    kc, vc = tc[:, :, -2], tc[:, :, -1]

    row_start = np.clip(np.arange(rows) - kr // 2, 0, rows - kr)
    row_off = row_start[:, None] + np.arange(kr)[None, :] - np.arange(rows)[:, None] + WIN_ROWS - 1
    col_start = np.clip(np.arange(GRID_W) - WIN_COLS // 2, 0, GRID_W - WIN_COLS)
    n_cb = GRID_W // COL_BLOCK
    band_start = np.minimum(col_start[::COL_BLOCK], GRID_W - COL_BAND)
    band_cols = band_start[:, None] + np.arange(COL_BAND)[None, :]
    qcol = np.arange(GRID_W).reshape(n_cb, COL_BLOCK)
    cs_q = col_start[qcol][:, :, None]
    col_mask = (band_cols[:, None, :] >= cs_q) & (band_cols[:, None, :] < cs_q + WIN_COLS)
    col_idx = np.clip(band_cols[:, None, :] - qcol[:, :, None] + WIN_COLS - 1, 0, 2 * WIN_COLS - 2)
    rpb_cols = rpb.astype(f32)[:, :, col_idx]
    n_win = kr * COL_BAND

    def row_fn(inp):
        q_row, rs, ro = inp
        kb = lax.dynamic_slice_in_dim(k, rs, kr, axis=1)[:, :, band_cols]
        vb = lax.dynamic_slice_in_dim(v, rs, kr, axis=1)[:, :, band_cols]
        qb = q_row.reshape(bsz, n_cb, COL_BLOCK, NA_HEADS, NA_HEAD_DIM)
        s_win = jnp.einsum('bmqhd,bamkhd->bhmqak', qb, kb).astype(f32)
        bias = jnp.transpose(rpb_cols[:, ro], (0, 2, 3, 1, 4))
        s_win = jnp.where(col_mask[:, :, None, :], s_win + bias, -jnp.inf)
        s_ctx = jnp.einsum('bmqhd,bkhd->bhmqk', qb, kc).astype(f32)
        s_all = jnp.concatenate([s_win.reshape(bsz, NA_HEADS, n_cb, COL_BLOCK, n_win), s_ctx], axis=-1)
        p = jax.nn.softmax(s_all, axis=-1).astype(v.dtype)
        p_win = p[..., :n_win].reshape(s_win.shape)
        o = (jnp.einsum('bhmqak,bamkhd->bmqhd', p_win, vb)
             + jnp.einsum('bhmqk,bkhd->bmqhd', p[..., n_win:], vc))
        return o.reshape(bsz, GRID_W, NA_WIDTH)

    o = lax.map(row_fn, (jnp.moveaxis(q, 1, 0), jnp.asarray(row_start, jnp.int32), jnp.asarray(row_off, jnp.int32)))
    out_l = jnp.moveaxis(o, 0, 1).reshape(bsz, l, NA_WIDTH) @ out_w

    out_c = None
    if need_ctx_out:
        qc = tc[:, :, 0] * qscale
        pc = jax.nn.softmax(jnp.einsum('bqhd,bkhd->bhqk', qc, kc).astype(f32), axis=-1).astype(vc.dtype)
        out_c = jnp.einsum('bhqk,bkhd->bqhd', pc, vc).reshape(hc.shape[0], hc.shape[1], NA_WIDTH) @ out_w
    return out_l, out_c

def setup_inputs(seed: int = 0) -> dict:
    key = jax.random.key(seed)
    ks = jax.random.split(key, 26)
    f32 = jnp.float32
    D = D_MODEL

    def nrm(k, shape, scale):
        return jax.random.normal(k, shape, f32) * scale

    dt0 = jnp.exp(jax.random.uniform(ks[14], (N_EVEN, 2, SSD_HEADS), f32, math.log(1e-3), math.log(1e-1)))
    return {
        'x': nrm(ks[0], (BATCH, SEQ, D), 1.0),
        'c': nrm(ks[1], (BATCH, D), 1.0),
        'ctx': nrm(ks[2], (BATCH, CTX_LEN, D), 1.0),
        'c_ctx': nrm(ks[3], (D,), 1.0),
        'ada_w': nrm(ks[4], (DEPTH, D, N_MOD * D), D ** -0.5),
        'ada_b': nrm(ks[5], (DEPTH, N_MOD * D), 0.02),
        'norm_g': 1.0 + nrm(ks[6], (DEPTH, 3, D), 0.1),
        'ffn_w1': nrm(ks[7], (DEPTH, 2, D, D_FF), D ** -0.5),
        'ffn_w3': nrm(ks[8], (DEPTH, 2, D, D_FF), D ** -0.5),
        'ffn_w2': nrm(ks[9], (DEPTH, 2, D_FF, D), D_FF ** -0.5),
        'ssd_in_w': nrm(ks[10], (N_EVEN, D, IN_A), D ** -0.5),
        'ssd_conv_w': nrm(ks[11], (N_EVEN, SSD_CONV, CONV_DIM), SSD_CONV ** -0.5),
        'ssd_conv_b': nrm(ks[12], (N_EVEN, CONV_DIM), 0.02),
        'ssd_dt_bias': dt0 + jnp.log(-jnp.expm1(-dt0)),
        'ssd_a_log': jnp.log(jax.random.uniform(ks[13], (N_EVEN, 2, SSD_HEADS), f32, 1.0, 16.0)),
        'ssd_d': 1.0 + nrm(ks[15], (N_EVEN, SSD_HEADS), 0.1),
        'ssd_norm_g': 1.0 + nrm(ks[16], (N_EVEN, SSD_INNER), 0.1),
        'pool_w': nrm(ks[17], (N_EVEN, N_POOL, POOL_GROUP, POOL_GROUP), POOL_GROUP ** -0.5),
        'pool_scale': 1.0 + nrm(ks[18], (N_EVEN, POOL_WIDTH), 0.1),
        'mix_a_out_w': nrm(ks[19], (N_EVEN, MIX_A_WIDTH, D), MIX_A_WIDTH ** -0.5),
        'na_qkv_w': nrm(ks[20], (N_ODD, D, 3 * NA_WIDTH), D ** -0.5),
        'na_rpb': nrm(ks[21], (N_ODD, NA_HEADS, 2 * WIN_ROWS - 1, 2 * WIN_COLS - 1), 0.2),
        'na_out_w': nrm(ks[22], (N_ODD, NA_WIDTH, D), NA_WIDTH ** -0.5),
        'final_norm_g': 1.0 + nrm(ks[23], (D,), 0.1),
    }

def reference(x, c, ctx, c_ctx, ada_w, ada_b, norm_g, ffn_w1, ffn_w3, ffn_w2, ssd_in_w, ssd_conv_w, ssd_conv_b,
              ssd_dt_bias, ssd_a_log, ssd_d, ssd_norm_g, pool_w, pool_scale, mix_a_out_w, na_qkv_w, na_rpb,
              na_out_w, final_norm_g):
    bsz = x.shape[0]
    xl, xc = x, ctx
    s_lat = jax.nn.silu(c)
    s_ctx = jax.nn.silu(c_ctx)
    for i in range(DEPTH):
        mod_l = (s_lat @ ada_w[i] + ada_b[i]).reshape(bsz, 1, N_MOD, D_MODEL)
        mod_c = (s_ctx @ ada_w[i] + ada_b[i]).reshape(N_MOD, D_MODEL)
        ml = [mod_l[:, :, j] for j in range(N_MOD)]
        mc = [mod_c[j] for j in range(N_MOD)]
        need_ctx = i < DEPTH - 1
        xl = xl + 0.5 * ml[2] * _swiglu(_modnorm(xl, norm_g[i, 0], ml[0], ml[1]), ffn_w1[i, 0], ffn_w3[i, 0], ffn_w2[i, 0])
        xc = xc + 0.5 * mc[2] * _swiglu(_modnorm(xc, norm_g[i, 0], mc[0], mc[1]), ffn_w1[i, 0], ffn_w3[i, 0], ffn_w2[i, 0])
        hl = _modnorm(xl, norm_g[i, 1], ml[3], ml[4])
        hc = _modnorm(xc, norm_g[i, 1], mc[3], mc[4])
        j = i // 2
        if i % 2 == 0:
            yl, yc = _ssd_pool_mixer(hl, hc, ssd_in_w[j], ssd_conv_w[j], ssd_conv_b[j], ssd_dt_bias[j], ssd_a_log[j],
                                     ssd_d[j], ssd_norm_g[j], pool_w[j], pool_scale[j], mix_a_out_w[j], need_ctx)
        else:
            yl, yc = _na_mixer(hl, hc, na_qkv_w[j], na_rpb[j], na_out_w[j], need_ctx)
        xl = xl + ml[5] * yl
        xl = xl + 0.5 * ml[8] * _swiglu(_modnorm(xl, norm_g[i, 2], ml[6], ml[7]), ffn_w1[i, 1], ffn_w3[i, 1], ffn_w2[i, 1])
        if need_ctx:
            xc = xc + mc[5] * yc
            xc = xc + 0.5 * mc[8] * _swiglu(_modnorm(xc, norm_g[i, 2], mc[6], mc[7]), ffn_w1[i, 1], ffn_w3[i, 1], ffn_w2[i, 1])
    return _rmsnorm(xl, final_norm_g)


_drawn_inputs = setup_inputs


def setup_inputs(seed=0):
    import zlib

    import numpy as np

    out = dict(_drawn_inputs(seed))
    spreads = {}
    factors = {'ssd_conv_b': 7.458, 'ssd_d': 8.0, 'na_rpb': 5.56}
    for name, (base, spread) in spreads.items():
        noise = np.random.default_rng([zlib.crc32(name.encode()), seed]).standard_normal(out[name].shape)
        drawn = base * np.exp(spread * noise) if base else spread * noise
        out[name] = __import__('jax').numpy.asarray(drawn.astype(out[name].dtype))
    for name, factor in factors.items():
        out[name] = (out[name] * factor).astype(out[name].dtype)
    return out
```

```python
from contextlib import ExitStack

import concourse.bass as bass
import concourse.mybir as mybir
from concourse.alu_op_type import AluOpType as ALU
import numpy as np

F32, F32R = mybir.dt.float32, mybir.dt.float32r
ACT = mybir.ActivationFunctionType
AX_X = mybir.AxisListType.X
ds = bass.ds

P = 128
D = 1024
KT = D // P
LAT, CTX = 256, 256
TOK = LAT + CTX
FF = 2816
FT = FF // P
HALF_FF = FF // 2
NMOD = 9
EPS = 1e-6
PAN = 4
LAG = 3
PANEL = 8 * P
HEADS = 16
HD = 64
GROUP_HEADS = 8
CHUNKS = TOK // P
CONV = 5
WINDOWS = (2, 4, 8, 16)
PAD = 8
NCONV = 12
ADA_COLS = 512
ADA_BLOCKS = NMOD * D // ADA_COLS
ADA_FIRST = 2 * D // ADA_COLS
GRID_W, WIN_C, ROWS = 64, 16, 4
RPB_R, RPB_C = 15, 31
NEG = -1.0e30

VEC_SIZES = [("c", 8), ("c_ctx", 8), ("norm_g", 48), ("ada_b", 144), ("conv_b", 12), ("conv_w", 60), ("gn_g", 8),
             ("pool_scale", 8), ("d_skip", 8), ("final_g", 8), ("dt_bias", 32), ("a_log", 32)]
VEC, _at = {}, 0
for _n, _s in VEC_SIZES:
    VEC[_n] = _at
    _at += _s
NVEC = _at


class Stage:

    def __init__(self, name, kind, iters, tokens=TOK, norm=None, arg=None, ada=0, ada_iters=0):
        self.name, self.kind, self.iters, self.tokens, self.norm, self.arg = name, kind, iters, tokens, norm, arg
        self.ada, self.ada_iters = ada, ada_iters
        if kind == "up":
            self.panels = [(0, 0, 8, 0, 0, 0, 0), (1, 0, 8, 0, 0, 1, 0), (0, 0, 8, P, 1, 0, 0), (1, 0, 8, P, 1, 1, 0)]
            self.outs = 2
        elif kind == "down":
            self.panels = [(s, k, n, 0, o, 0, 11 * s + k) for o in range(2) for s in range(2)
                           for k, n in ((0, 6), (6, 5))]
            self.outs = 2
        elif kind == "mix":
            self.panels = [(s, 0, 8, P * o, o, 0, 8 * s) for o in range(2) for s in range(2)]
            self.outs = 2
        else:
            self.panels = [(o // 2, 0, 8, P * (o % 2), o, 0, 0) for o in range(4)]
            self.outs = 4
        self.groups = len(self.panels) // PAN

    def opens(self, j):
        return j == 0 or self.panels[j][4:6] != self.panels[j - 1][4:6] or self.kind == "up"

    def closes(self, j):
        last = j + 1 == len(self.panels) or self.panels[j + 1][4] != self.panels[j][4]
        return self.panels[j][4] if last else None

    def slab_ends(self, slot):
        return max(j for j in range(PAN) if self.panels[j][0] == slot)


STAGES = [
    Stage("ffn0_up", "up", 11, norm=0, arg=(0, 0), ada=4, ada_iters=11), Stage("ffn0_down", "down", 4, arg=(0, 0)),
    Stage("xbc", "lin", 3, norm=1, arg=1024), Stage("pool_in", "lin", 2, arg=2592), Stage("z", "lin", 2, arg=0),
    Stage("mix_out", "mix", 4),
    Stage("ffn1_up", "up", 11, norm=2, arg=(0, 1), ada=16, ada_iters=11), Stage("ffn1_down", "down", 4, arg=(0, 1)),
    Stage("ffn2_up", "up", 11, norm=3, arg=(1, 0), ada=27, ada_iters=9), Stage("ffn2_down", "down", 4, arg=(1, 0)),
    Stage("k", "lin", 2, norm=4, arg=1024), Stage("v", "lin", 2, arg=2048), Stage("q", "lin", 2, tokens=LAT, arg=0),
    Stage("na_out", "lin", 2, tokens=LAT, arg=0),
    Stage("ffn3_up", "up", 11, tokens=LAT, norm=5, arg=(1, 1)), Stage("ffn3_down", "down", 4, tokens=LAT, arg=(1, 1)),
]
RUN = STAGES
_p = _o = _g = _u = 0
for _i, _s in enumerate(STAGES):
    _s.index, _s.panel0, _s.out0, _s.group0, _s.up0 = _i, _p, _o, _g, _u
    _s.bank0 = 4 * (_i % 2)
    _p += len(_s.panels) * _s.iters
    _o += _s.outs * _s.iters
    _g += _s.groups * _s.iters
    _u += _s.outs * _s.iters if _s.kind == "up" else 0
BY = {s.name: s for s in STAGES}
UPDATES = [s for s in STAGES if s.kind in ("down", "mix") or s.name == "na_out"]
for _i, _s in enumerate(UPDATES):
    _s.update = _i + 1
FWD_ORDER, BWD_ORDER = (2, 3, 0, 1), (3, 2, 1, 0)
ORDER = (FWD_ORDER, BWD_ORDER)
UNITS = [(g, c, quad, d) for g in range(2) for c in range(CHUNKS) for quad in range(2) for d in range(2)]


def build(nc, x, ctx_in, vec_in, const_in, inv_in, ada_w, w1, w3, w2, in_w, pool_w, mix_w, qkv_w, rpb, na_w, out):
    ctx = ExitStack()
    with ctx:
        base = [16512]

        def at(name, shape, dt=F32, offset=None):
            size = 4
            for s in shape[1:]:
                size *= s
            if offset is None:
                offset = base[0]
                base[0] += size
            return nc.alloc_sbuf_tensor_at(name, shape, dt, offset=offset)

        def sem(name):
            return ctx.enter_context(nc.semaphore(name))

        trunk = at("trunk", [P, KT, TOK])
        h_at = base[0]
        h_hi = at("h_hi", [P, KT, TOK], F32R)
        h_lo = at("h_lo", [P, KT, TOK], F32R)
        g_at = base[0]
        g_hi = at("g_hi", [P, FT, TOK], F32R)
        g_lo = at("g_lo", [P, FT, TOK], F32R)
        raw = [at(f"raw{i}", [P, 2048]) for i in range(2)]
        ada_at = base[0]
        ada_raw = [at(f"ada_raw{i}", [P, 2, ADA_COLS]) for i in range(2)]
        pan_hi = [at(f"pan_hi{i}", [P, 8, P], F32R) for i in range(PAN)]
        pan_lo = [at(f"pan_lo{i}", [P, 8, P], F32R) for i in range(PAN)]
        acc_at = base[0]
        ada_acc = at("ada_acc", [P, 2, ADA_COLS])
        vec = at("vec", [P, NVEC])
        mods = at("mods", [P, 2 * NMOD * KT, 2])
        norm_scale = at("norm_scale", [P, KT, 2])
        gate = at("gate", [P, KT, 2])
        cond = at("cond", [P, 2, KT])
        ident = at("ident", [P, P])
        na_mask = at("na_mask", [P, GRID_W])
        ones = at("ones", [P, P])
        tmp = [at(f"tmp{i}", [P, TOK]) for i in range(2)]
        ssq = at("ssq", [P, TOK])
        eps_end = base[0]
        assert eps_end <= 229344, eps_end

        f = 4
        x_in = at("x_in", [P, 4, D], offset=g_at)
        ada_first = at("ada_first", [P, ADA_FIRST, KT, ADA_COLS], offset=g_at + 4096 * f)
        ada_rows = at("ada_rows", [2, ADA_FIRST, ADA_COLS], offset=g_at + 20480 * f)
        pooled_hi = at("pooled_hi", [P, KT, TOK], F32R, offset=g_at)
        pooled_lo = at("pooled_lo", [P, KT, TOK], F32R, offset=g_at + 4096 * f)
        xbc = at("xbc", [P, NCONV, TOK], offset=g_at + 8192 * f)
        zs_at = g_at + 14336 * f
        zs = at("zs", [P, KT, TOK], offset=zs_at)
        conv_pad = [at(f"conv_pad{i}", [P, 2, LAT + 4], offset=zs_at + i * 520 * f) for i in range(2)]
        pw_len = LAT + 2 * PAD
        pool_u = at("pool_u", [P, 2, pw_len], offset=zs_at)
        pool_s = [at(f"pool_s{i}", [P, 2, pw_len], offset=zs_at + (i + 1) * 2 * pw_len * f) for i in range(2)]
        inv_count = at("inv_count", [P, 4, LAT], offset=zs_at + 1664 * f)
        dt_raw = at("dt_raw", [P, KT, 32], offset=zs_at + 2688 * f)
        dt_hi = at("dt_hi", [P, KT, 32], F32R, offset=zs_at + 2944 * f)
        dt_lo = at("dt_lo", [P, KT, 32], F32R, offset=zs_at + 3200 * f)
        st_at = g_at + 18432 * f
        pool_wt = at("pool_wt", [P, 4, 2, 2 * P], offset=st_at)
        mu = at("mu", [P, 4, TOK], offset=st_at + 2048 * f)
        b_tok = at("b_tok", [P, CHUNKS, P], offset=st_at)
        states = [at(f"state{d}", [P, 3, 512], offset=st_at + (512 + d * 1536) * f) for d in range(2)]
        xd = [at(f"xd{d}", [P, CHUNKS, 512], offset=h_at + d * 2048 * f) for d in range(2)]
        seg_rhs = [at(f"seg_rhs{i}", [P, 4, P], offset=h_at + (4096 + 512 * i) * f) for i in range(2)]
        decay = [at(f"decay{i}", [P, 4, P], offset=h_at + (5120 + 512 * i) * f) for i in range(2)]
        weight = [at(f"weight{i}", [P, 4, P], offset=h_at + (6144 + 512 * i) * f) for i in range(2)]
        xdd = [at(f"xdd{i}", [P, 512], offset=h_at + (7168 + 512 * i) * f) for i in range(2)]
        y_hi = at("y_hi", [P, KT, TOK], F32R, offset=h_at)
        y_lo = at("y_lo", [P, KT, TOK], F32R, offset=h_at + 4096 * f)
        tri = at("tri", [P, 4, P], offset=ada_at)
        cb = [at(f"cb{d}", [P, CHUNKS, P], offset=ada_at + (512 + 512 * d) * f) for d in range(2)]
        exps = at("exps", [P, 3, CHUNKS, 32], offset=ada_at + 1536 * f)
        dt_x = at("dt_x", [P, CHUNKS, 32], offset=acc_at)
        dt_a = at("dt_a", [P, CHUNKS, 32], offset=acc_at + 128 * f)
        dt_b = at("dt_b", [P, CHUNKS, 32], offset=acc_at + 256 * f)
        dt_c = at("dt_c", [P, CHUNKS, 32], offset=acc_at + 384 * f)
        dt = at("dt", [P, CHUNKS, 32], offset=acc_at + 512 * f)
        dta = at("dta", [P, CHUNKS, 32], offset=acc_at + 640 * f)
        a_coef = at("a_coef", [P, 32], offset=acc_at + 768 * f)
        kt_all = at("kt_all", [P, KT, TOK], offset=g_at)
        vt_all = at("vt_all", [P, KT, TOK], offset=g_at + 4096 * f)
        o_hi = at("o_hi", [P, KT, LAT], F32R, offset=g_at + 4096 * f)
        o_lo = at("o_lo", [P, KT, LAT], F32R, offset=g_at + 6144 * f)
        qt_all = at("qt_all", [P, KT, LAT], offset=g_at + 8192 * f)
        v_tok = at("v_tok", [P, 4, D], offset=g_at + 10240 * f)
        bias_rev = at("bias_rev", [P, HEADS, ROWS, GRID_W], offset=g_at + 10240 * f)
        bias = at("bias", [P, 2, HEADS, ROWS, GRID_W], offset=g_at + 14336 * f)
        q_s = [at(f"q_s{i}", [P, LAT], offset=h_at + 256 * i * f) for i in range(2)]
        k_s = [at(f"k_s{i}", [P, TOK], offset=h_at + (512 + 512 * i) * f) for i in range(2)]
        v_s = at("v_s", [P, 4, P], offset=h_at + 1536 * f)
        score = [at(f"score{i}", [P, 4, TOK], offset=h_at + (2048 + 2048 * i) * f) for i in range(2)]
        prob_t = [at(f"prob_t{i}", [P, 4, LAT], offset=h_at + (6144 + 1024 * i) * f) for i in range(2)]
        smax = at("smax", [P, 4, 4], offset=acc_at)
        y_out = at("y_out", [P, KT, LAT], offset=g_at)
        y_tok = at("y_tok", [P, 2, D], offset=g_at + 2048 * f)

        ps = [ctx.enter_context(nc.psum_tensor(f"bank{i}", [P, 512], F32)) for i in range(8)]
        ada_bank, stat_bank = ps[6], ps[7]

        vec_loaded, const_loaded, x_loaded, mask_loaded = (sem(n) for n in ("vec_loaded", "const_loaded", "x_loaded",
                                                                           "mask_loaded"))
        raw_loaded = [sem(f"raw_loaded{i}") for i in range(2)]
        ada_loaded = [sem(f"ada_loaded{i}") for i in range(2)]
        mixer_loaded, tri_loaded = sem("mixer_loaded"), sem("tri_loaded")
        bias_loaded = sem("bias_loaded")
        hi_done, lo_done = sem("hi_done"), sem("lo_done")
        panel_used = sem("panel_used")
        out_taken = sem("out_taken")
        silu_done, g_hi_done, g_ready = sem("silu_done"), sem("g_hi_done"), sem("g_ready")
        square_done, ssq_added = sem("square_done"), sem("ssq_added")
        stat_done, var_done, root_done = sem("stat_done"), sem("var_done"), sem("root_done")
        normed, h_hi_done, h_ready = sem("normed"), sem("h_hi_done"), sem("h_ready")
        ada_step, ada_summed, mods_done = sem("ada_step"), sem("ada_summed"), sem("mods_done")
        cond_done, ones_done = sem("cond_done"), sem("ones_done")
        x_turned, x_taken = sem("x_turned"), sem("x_taken")
        first_loaded = [sem(f"first_loaded{b}") for b in range(ADA_FIRST)]
        rows_mm, rows_taken, rows_turned = sem("rows_mm"), sem("rows_taken"), sem("rows_turned")
        dve_link = sem("dve_link")
        act_link = sem("act_link")
        conv_step, conv_done = sem("conv_step"), sem("conv_done")
        dt_split, dt_mm, dt_taken, dt_act, dt_vec = (sem(n) for n in ("dt_split", "dt_mm", "dt_taken", "dt_act",
                                                                      "dt_vec"))
        mu_ready, pool_mm, pool_hi, pool_lo = sem("mu_ready"), sem("pool_mm"), sem("pool_hi"), sem("pool_lo")
        z_done = sem("z_done")
        dt_abs, dt_hi_done = sem("dt_abs"), sem("dt_hi_done")
        sums_mm, exps_done = sem("sums_mm"), sem("exps_done")
        xt_mm, xd_done, bt_mm, bt_done, cb_mm, cb_done = (sem(n) for n in ("xt_mm", "xd_done", "bt_mm", "bt_done",
                                                                          "cb_mm", "cb_done"))
        xdd_done, state_mm, state_done = sem("xdd_done"), sem("state_mm"), sem("state_done")
        seg_ready, seg_mm, decay_done, weight_done, diag_mm = (sem(n) for n in ("seg_ready", "seg_mm", "decay_done",
                                                                               "weight_done", "diag_mm"))
        off_mm, y_sum, yt_mm, yt_done = sem("off_mm"), sem("y_sum"), sem("yt_mm"), sem("yt_done")
        y_gated, y_hi_done, y_ready = sem("y_gated"), sem("y_hi_done"), sem("y_ready")
        gn_square, gn_added, gn_stat, gn_var, gn_root = (sem(n) for n in ("gn_square", "gn_added", "gn_stat",
                                                                         "gn_var", "gn_root"))
        vt_mm, vt_done = sem("vt_mm"), sem("vt_done")
        masked, q_staged, v_staged, qk_mm = sem("masked"), sem("q_staged"), sem("v_staged"), sem("qk_mm")
        s_ctx, s_done, p_done, p_norm = sem("s_ctx"), sem("s_done"), sem("p_done"), sem("p_norm")
        pt_mm, pt_act, pt_dve, pv_mm, o_hi_done, o_done = (sem(n) for n in ("pt_mm", "pt_act", "pt_dve", "pv_mm",
                                                                           "o_hi_done", "o_done"))
        max_done, max_found, sum_inverted = sem("max_done"), sem("max_found"), sem("sum_inverted")
        f_normed, f_turned, stored = sem("f_normed"), sem("f_turned"), sem("stored")
        f_taken_dve, f_taken_act = sem("f_taken_dve"), sem("f_taken_act")

        block = ctx.enter_context(nc.Block())

        def panel(S, i, j):
            return i * len(S.panels) + (S.panel0 + j)

        def output(S, i, o):
            return i * S.outs + (S.out0 + o)

        def bank(S, j):
            p = S.panels[j]
            return ps[S.bank0 + (2 * p[4] + p[5] if S.kind == "up" else p[4])]

        def walk(eng, step):
            def iteration(S, i, first):
                for j in range(len(S.panels)):
                    q = j - LAG
                    if q >= 0:
                        R, ri = S, i
                    elif not first:
                        R, ri, q = S, i - 1, len(S.panels) + q
                    else:
                        R = RUN[S.index - 1] if S.index else None
                        ri, q = (R.iters - 1, len(R.panels) + q) if R else (0, 0)
                    o = R.closes(q) if R else None
                    step(S, i, j, (R, ri, o) if o is not None else None, first)

            for S in RUN:
                iteration(S, 0, True)
                cuts = [1, S.iters] if not 0 < S.ada_iters < S.iters else [1, S.ada_iters, S.ada_iters + 1, S.iters]
                for a, b in zip(cuts, cuts[1:]):
                    if b - a <= 1:
                        for i in range(a, b):
                            iteration(S, i, False)
                    else:
                        with eng.Fori(a, b) as i:
                            iteration_in_loop(S, i, a, iteration)
            last = RUN[-1]
            for q in range(LAG):
                o = last.closes(len(last.panels) - LAG + q)
                step(None, 0, q, (last, last.iters - 1, o) if o is not None else None, True)

        def head_pairs(eng, step):
            with eng.Fori(0, KT // 2 - 1) as m:
                for b in range(2):
                    step(m * 2 + b, b, True)
            step(KT - 2, 0, True)
            step(KT - 1, 1, False)

        def silu_first(S, j, first):
            return S is not None and S.kind == "up" and S.tokens == LAT and j == 0 and not first

        def iteration_in_loop(S, i, a, iteration):
            S.at = a
            iteration(S, i, False)

        @block.sync
        def _(sp):
            sp.dma_start(vec[:], vec_in).then_inc(vec_loaded, 16)
            sp.dma_start(x_in[:, 0:2, :], x.rearrange("b (c p) d -> p (b c) d", p=P)).then_inc(x_loaded, 16)
            sp.dma_start(x_in[:, 2:4, :], ctx_in.rearrange("b (c p) d -> p (b c) d", p=P)).then_inc(x_loaded, 16)
            sp.dma_start(ident[:], const_in[:, 0:P]).then_inc(const_loaded, 16)
            for b in range(ADA_FIRST):
                src = ada_w[0][:, b * ADA_COLS:(b + 1) * ADA_COLS]
                sp.dma_start(ada_first[:, b], src.rearrange("(k p) m -> p k m", p=P)).then_inc(first_loaded[b], 16)
            sp.dma_start(na_mask[:], const_in[:, P:P + GRID_W]).then_inc(mask_loaded, 16)

            def slab(S, i, group, s):
                if S.kind == "up":
                    w = (w1, w3)[s][S.arg[0], S.arg[1]]
                    src = w[:, ds(i * 2 * P, 2 * P)].rearrange("(k p) m -> p k m", p=P)
                elif S.kind == "down":
                    w = w2[S.arg[0], S.arg[1]]
                    src = w[s * HALF_FF:(s + 1) * HALF_FF, ds(i * 2 * P + group * P, P)]
                    src = src.rearrange("(k p) m -> p k m", p=P)
                elif S.kind == "mix":
                    src = mix_w[0][s * D:(s + 1) * D, ds(i * 2 * P, 2 * P)].rearrange("(k p) m -> p k m", p=P)
                else:
                    w = in_w[0] if S.name in ("xbc", "pool_in", "z") else na_w[0] if S.name == "na_out" else qkv_w[0]
                    src = w[:, ds(i * 4 * P + (S.arg + s * 2 * P), 2 * P)].rearrange("(k p) m -> p k m", p=P)
                return src

            def group_loads(S, i, group, before, bi):
                for s in range(2):
                    if before is not None:
                        sp.wait_ge(lo_done, bi + (before.slab_ends(s) + 1 + PAN))
                    cols = P if S.kind == "down" else 2 * P
                    k = 11 if S.kind == "down" else 8
                    dst = raw[s][:, 0:k * cols].rearrange("p (k m) -> p k m", k=k)
                    sp.dma_start(dst, slab(S, i, group, s)).then_inc(raw_loaded[s], 16)

            def stage_loads(S, i, first):
                for group in range(S.groups):
                    if first and group == 0:
                        B = RUN[S.index - 1] if S.index else None
                        group_loads(S, i, group, B, S.panel0 - PAN)
                    else:
                        group_loads(S, i, group, S, panel(S, i, group * PAN - PAN))

            for S in RUN:
                stage_loads(S, 0, True)
                if S.name == "xbc":
                    sp.wait_ge(panel_used, S.panel0 + PAN)
                    sp.dma_start(inv_count[:], inv_in.rearrange("p (w t) -> p w t", w=4)).then_inc(mixer_loaded, 16)
                    sp.dma_start(dt_raw[:], in_w[0][:, 2560:2592].rearrange("(k p) m -> p k m", p=P)
                                 ).then_inc(mixer_loaded, 16)
                    sp.dma_start(pool_wt[:], pool_w[0].rearrange("g (k p) m -> p g k m", p=P)
                                 ).then_inc(mixer_loaded, 16)
                    sp.wait_ge(ada_summed, 16)
                    sp.dma_start(tri[:], const_in[:, P + GRID_W:].rearrange("p (a b) -> p a b", a=4)
                                 ).then_inc(tri_loaded, 16)
                if S.iters <= 2:
                    for i in range(1, S.iters):
                        stage_loads(S, i, False)
                else:
                    with sp.Fori(1, S.iters) as i:
                        stage_loads(S, i, False)
            sp.wait_ge(f_taken_dve, 2)
            sp.wait_ge(f_taken_act, 2)
            sp.dma_start(out.rearrange("b (c p) d -> p (b c) d", p=P), y_tok[:]).then_inc(stored, 16)
            sp.wait_ge(stored, 16)

        @block.gpsimd
        def _(pool):
            def ada_quarters(layer, b, n):
                for q in range(4):
                    pool.wait_ge(ada_step, n * 4 + (4 * q + 4))
                    src = ada_w[layer, q * 2 * P:(q + 1) * 2 * P, ds(b * ADA_COLS, ADA_COLS)]
                    pool.dma_start(ada_raw[q % 2][:], src.rearrange("(k p) m -> p k m", p=P)
                                   ).then_inc(ada_loaded[q % 2], 16)

            pool.wait_ge(first_loaded[ADA_FIRST - 1], 16)
            with pool.Fori(ADA_FIRST, 16) as b:
                ada_quarters(0, b, b * 4)
            if len(RUN) > BY["ffn1_up"].index:
                pool.wait_ge(out_taken, BY["ffn1_up"].out0 + PAN)
                with pool.Fori(16, 18) as b:
                    ada_quarters(0, b, b * 4)
                with pool.Fori(0, 9 if len(RUN) <= BY["ffn2_up"].index else 18) as b:
                    ada_quarters(1, b, b * 4 + 18 * 4)
            if len(RUN) > BY["na_out"].index:
                pool.wait_ge(panel_used, BY["k"].panel0 + PAN)
                for t in range(2):
                    if t:
                        pool.wait_ge(masked, 1)
                    for r in range(2):
                        row = 2 * t + r
                        for key_row in range(ROWS):
                            src = bass.AP(tensor=rpb.tensor,
                                          offset=(key_row - row + 7) * RPB_C + WIN_C - GRID_W,
                                          ap=[[1, GRID_W], [RPB_R * RPB_C, HEADS], [1, GRID_W]])
                            pool.dma_start(bias_rev[r * GRID_W:(r + 1) * GRID_W, :, key_row, :], src
                                           ).then_inc(bias_loaded, 16)
                pool.wait_ge(out_taken, BY["na_out"].out0 + PAN)
                pool.wait_ge(panel_used, BY["na_out"].panel0 + PAN)
                pool.wait_ge(vt_done, 8)

                def stage_qk(t, b):
                    if not (isinstance(t, int) and t < 2):
                        pool.wait_ge(qk_mm, t * 4 - 4 + 1)
                    nc.gpsimd.tensor_copy(q_s[b][:], qt_all[:, ds(t, 1), :].rearrange("p a b -> p (a b)")
                                          ).then_inc(q_staged, 1)
                    nc.gpsimd.tensor_copy(k_s[b][:], kt_all[:, ds(t, 1), :].rearrange("p a b -> p (a b)")
                                          ).then_inc(q_staged, 1)

                def staging(t, b, more):
                    if more:
                        stage_qk(t + 1, 1 - b)
                    pool.wait_ge(pv_mm, t * 2 + 2)
                    nc.gpsimd.tensor_copy(v_s[:], v_tok[:, :, ds(t * P, P)]).then_inc(v_staged, 1)

                stage_qk(0, 0)
                head_pairs(pool, staging)

        @block.tensor
        def _(pe):
            pe.sem_inc(panel_used, PAN)
            pe.sem_inc(qk_mm, 1)
            pe.sem_inc(pv_mm, 2)
            pe.sem_inc(pt_mm, 4)
            pe.sem_inc(ada_summed, ADA_FIRST)

            def run_panel(S, i, j, first):
                slot, _, nk, _, o, part, k0 = S.panels[j]
                gp = panel(S, i, j)
                N = S.tokens
                acts = (g_hi, g_lo) if S.kind == "down" else (h_hi, h_lo)
                if S.opens(j) and part == 0:
                    pe.wait_ge(out_taken, output(S, i, o) - S.outs + (1 + PAN))
                pe.wait_ge(lo_done, gp + (1 + PAN))
                dst = bank(S, j)[:, 0:N]
                ends = S.closes(j) is not None or S.kind == "up"
                for k in range(nk):
                    gk = k0 + k
                    if S.kind == "mix":
                        acts = (y_hi, y_lo) if gk < KT else (pooled_hi, pooled_lo)
                    elif S.name == "na_out":
                        acts = (o_hi, o_lo)
                    a_hi, a_lo = acts[0][:, gk % KT if S.kind == "mix" else gk, 0:N], \
                        acts[1][:, gk % KT if S.kind == "mix" else gk, 0:N]
                    if first and o == 0 and part == 0:
                        if S.norm is not None:
                            pe.wait_ge(h_ready, KT * S.norm + gk + 1)
                        elif S.kind == "down":
                            pe.wait_ge(g_ready, RUN[S.index - 1].up0 + gk + 2)
                        elif S.kind == "mix" and gk < KT:
                            pe.wait_ge(y_ready, gk + 1)
                    w_hi, w_lo = pan_hi[j % PAN][:, k, :], pan_lo[j % PAN][:, k, :]
                    start = S.opens(j) and k == 0
                    stop = ends and k == nk - 1
                    pe.matmul(dst, w_hi, a_hi, start=start, stop=False)
                    pe.matmul(dst, w_hi, a_lo, start=False, stop=False)
                    mm = pe.matmul(dst, w_lo, a_hi, start=False, stop=stop)
                mm.then_inc(panel_used, 1)

            def ada_sum(b):
                pe.wait_ge(ada_step, b * 16 + (16 + 8))
                pe.wait_ge(mods_done, b + 1)
                for ct in range(4):
                    for v in range(2):
                        mm = pe.matmul(ada_bank[:, 2 * ct + v:2 * ct + v + 1], ada_acc[:, v, ct * P:(ct + 1) * P],
                                       ones[:, 0:1], start=True, stop=True)
                mm.then_inc(ada_summed, 1)

            def stat(n, N):
                pe.wait_ge(ssq_added, KT * (n + 1) + 1)
                pe.matmul(stat_bank[:, 0:N], ones[:], ssq[:, 0:N], start=True, stop=True).then_inc(stat_done, 1)

            def dt_products():
                pe.wait_ge(dt_split, 1)
                for c in range(CHUNKS):
                    dst = ps[7][:, c * 32:c * 32 + 32]
                    for k in range(KT):
                        a_hi, a_lo = h_hi[:, k, c * P:(c + 1) * P], h_lo[:, k, c * P:(c + 1) * P]
                        pe.matmul(dst, a_hi, dt_hi[:, k, :], start=k == 0, stop=False)
                        pe.matmul(dst, a_hi, dt_lo[:, k, :], start=False, stop=False)
                        mm = pe.matmul(dst, a_lo, dt_hi[:, k, :], start=False, stop=k == KT - 1)
                mm.then_inc(dt_mm, 1)

            def pool_products(g0, banks):
                for g in (g0, g0 + 1):
                    pe.wait_ge(mu_ready, 2 * g + 2)
                    for t in range(2):
                        for k in range(2):
                            mm = pe.matmul(ps[banks + 2 * (g - g0) + t][:], pool_wt[:, g, k, t * P:(t + 1) * P],
                                           mu[:, 2 * (g % 2) + k, :], start=k == 0, stop=k == 1)
                        mm.then_inc(pool_mm, 1)

            def turn(dst, src):
                return pe.transpose(dst, src, ident[:])

            def ssd():
                pe.wait_ge(dt_vec, 1)
                pe.wait_ge(tri_loaded, 16)
                pe.wait_ge(out_taken, BY["mix_out"].out0 + PAN)
                pe.wait_ge(pool_lo, 8)
                for which in range(3):
                    for c in range(CHUNKS):
                        for d in range(2):
                            lhs = (tri[:, d, :], tri[:, 2 + d, :], ones[:])[which]
                            at0 = which * P + c * 32 + d * HEADS
                            mm = pe.matmul(ps[4][:, at0:at0 + HEADS], lhs, dta[:, c, d * HEADS:(d + 1) * HEADS],
                                           start=True, stop=True)
                mm.then_inc(sums_mm, 1)
                u = yt = 0
                for g in range(2):
                    for c in range(CHUNKS):
                        pe.wait_ge(conv_done, NCONV + 2)
                        if g or c > 1:
                            pe.wait_ge(xd_done, 2 * (CHUNKS * g + c - 1))
                        for t in range(4):
                            mm = turn(ps[5 + c % 2][:, t * P:(t + 1) * P], xbc[:, 4 * g + t, c * P:(c + 1) * P])
                        mm.then_inc(xt_mm, 1)
                    if g == 0:
                        pe.wait_ge(exps_done, 1)
                    else:
                        pe.wait_ge(yt_done, CHUNKS)
                    for c in range(CHUNKS):
                        mm = turn(ps[4][:, c * P:(c + 1) * P], xbc[:, 8 + g, c * P:(c + 1) * P])
                    mm.then_inc(bt_mm, 1)
                    for c in range(CHUNKS):
                        mm = pe.matmul(ps[7][:, c * P:(c + 1) * P], xbc[:, 8 + g, c * P:(c + 1) * P],
                                       xbc[:, 10 + g, c * P:(c + 1) * P], start=True, stop=True)
                    mm.then_inc(cb_mm, 1)
                    pe.wait_ge(bt_done, g + 1)
                    pe.wait_ge(xd_done, 8 * (g + 1))
                    for n in range(6):
                        pos, d = n // 2, n % 2
                        c = ORDER[d][pos]
                        pe.wait_ge(xdd_done, 6 * g + n + 1)
                        if n > 1:
                            pe.wait_ge(state_done, 6 * g + n - 1)
                        pe.matmul(ps[5 + n % 2][:], b_tok[:, c, :], xdd[n % 2][:], start=True, stop=True
                                  ).then_inc(state_mm, 1)
                    pe.wait_ge(cb_done, 2 * (g + 1))
                    pe.wait_ge(state_done, 6 * (g + 1))
                    for c in range(CHUNKS):
                        if g or c:
                            pe.wait_ge(y_sum, CHUNKS * g + c)
                        for d in range(2):
                            pos = ORDER[d].index(c)
                            if pos:
                                mm = pe.matmul(ps[6 + d][:], xbc[:, 10 + g, c * P:(c + 1) * P],
                                               states[d][:, pos - 1, :], start=True, stop=True)
                        mm.then_inc(off_mm, 1)
                        for n in range(4):
                            quad, d = n // 2, n % 2
                            pe.wait_ge(seg_ready, u + 1)
                            if u > 1:
                                pe.wait_ge(decay_done, u - 1)
                            pe.matmul(ps[u % 2][:], tri[:, 2 + d, :], seg_rhs[u % 2][:].rearrange("p a b -> p (a b)"),
                                      start=True, stop=True).then_inc(seg_mm, 1)
                            if n:
                                diagonal(u - 1, n - 1, c)
                            u += 1
                        diagonal(u - 1, 3, c)
                        pe.wait_ge(y_sum, CHUNKS * g + c + 1)
                        if c or g:
                            pe.wait_ge(yt_done, CHUNKS * g + c)
                        for t in range(4):
                            mm = turn(ps[4][:, t * P:(t + 1) * P], tmp[0][:, t * P:(t + 1) * P])
                        mm.then_inc(yt_mm, 1)

            def diagonal(u, n, c):
                quad, d = n // 2, n % 2
                pe.wait_ge(weight_done, u + 1)
                for hh in range(4):
                    hx = 4 * quad + hh
                    mm = pe.matmul(ps[2 + c % 2][:, hx * HD:(hx + 1) * HD], weight[u % 2][:, hh, :],
                                   xd[d][:, c, hx * HD:(hx + 1) * HD], start=n == 0 and hh == 0,
                                   stop=n == 3 and hh == 3, skip_group_check=True)
                mm.then_inc(diag_mm, 1)

            def attention():
                for t in range(KT):
                    pe.wait_ge(out_taken, BY["v"].out0 + BY["v"].outs * BY["v"].iters + PAN)
                    if t > 1:
                        pe.wait_ge(vt_done, t - 1)
                    for c in range(4):
                        mm = turn(ps[4 + t % 2][:, c * P:(c + 1) * P], vt_all[:, t, c * P:(c + 1) * P])
                    mm.then_inc(vt_mm, 1)
                pe.wait_ge(out_taken, BY["na_out"].out0 + PAN)
                pe.wait_ge(vt_done, 8)

                def scores(t, b, n):
                    a, qt = n // 2, n % 2
                    pe.wait_ge(q_staged, t * 2 + 2)
                    pe.wait_ge(s_ctx, t * 4 + (n + 1))
                    pe.wait_ge(s_done, t * 4 + (n + 1))
                    pe.matmul(ps[n][:], q_s[b][a * HD:(a + 1) * HD, qt * P:(qt + 1) * P],
                              k_s[b][a * HD:(a + 1) * HD, :], start=True, stop=True).then_inc(qk_mm, 1)

                def pair(t, b, more):
                    for a in range(2):
                        pe.wait_ge(pt_act, t * 2 + (a + 1))
                        pe.wait_ge(pt_dve, t * 2 + (a + 1))
                        for qt in range(2):
                            pe.wait_ge(p_norm, t * 4 + (2 * a + qt + 1))
                            for kt in range(4):
                                dst = ps[4 + kt // 2][:, (kt % 2) * LAT + qt * P:(kt % 2) * LAT + (qt + 1) * P]
                                mm = turn(dst, score[b][:, 2 * a + qt, kt * P:(kt + 1) * P])
                        mm.then_inc(pt_mm, 1)
                        if more:
                            scores(t + 1, 1 - b, 2 * a)
                            scores(t + 1, 1 - b, 2 * a + 1)
                        pe.wait_ge(pt_act, t * 2 + (a + 2))
                        pe.wait_ge(pt_dve, t * 2 + (a + 2))
                        if a == 0:
                            pe.wait_ge(v_staged, t + 1)
                            pe.wait_ge(o_done, t + 1)
                        for kt in range(4):
                            mm = pe.matmul(ps[6][a * HD:(a + 1) * HD, 0:LAT], v_s[:, kt, a * HD:(a + 1) * HD],
                                           prob_t[a][:, kt, :], start=kt == 0, stop=kt == 3)
                        mm.then_inc(pv_mm, 1)

                for n in range(4):
                    scores(0, 0, n)
                head_pairs(pe, pair)

            pe.wait_ge(x_loaded, 32)
            pe.wait_ge(const_loaded, 16)
            for t in range(KT):
                if t > 1:
                    pe.wait_ge(x_taken, t - 1)
                for c in range(4):
                    mm = turn(ps[t % 2][:, c * P:(c + 1) * P], x_in[:, c, t * P:(t + 1) * P])
                mm.then_inc(x_turned, 1)
            pe.wait_ge(ones_done, 1)
            stat(0, TOK)
            pe.wait_ge(cond_done, 1)
            for b in range(ADA_FIRST):
                pe.wait_ge(first_loaded[b], 16)
                for k in range(KT):
                    mm = pe.matmul(ps[2 + b][0:2, :], cond[:, :, k], ada_first[:, b, k, :],
                                   start=k == 0, stop=k == KT - 1)
                mm.then_inc(rows_mm, 1)
            for b in range(ADA_FIRST):
                pe.wait_ge(rows_taken, b + 1)
                for t in range(4):
                    c = 4 * b + t
                    mm = pe.transpose(ada_bank[:, 2 * c:2 * c + 2], ada_rows[:, b, t * P:(t + 1) * P], ident[0:2, 0:2])
            mm.then_inc(rows_turned, 1)
            for S in RUN:
                if S.norm:
                    stat(S.norm, LAT if S.norm == 5 else TOK)
                if S.name == "z":
                    pe.wait_ge(out_taken, BY["pool_in"].out0 + PAN)
                    pool_products(0, 0)
                    pe.wait_ge(pool_lo, 4)
                if S.name == "pool_in":
                    dt_products()
                if S.name == "mix_out":
                    pe.wait_ge(out_taken, BY["z"].out0 + PAN)
                    pool_products(2, 4)
                    ssd()
                    pe.wait_ge(gn_added, 8)
                    pe.matmul(stat_bank[:], ones[:], ssq[:], start=True, stop=True).then_inc(gn_stat, 1)
                if S.name == "na_out":
                    attention()
                    pe.wait_ge(o_done, 9)
                for j in range(len(S.panels)):
                    if S.name == "pool_in" and j == 3:
                        pe.wait_ge(dt_taken, 1)
                    run_panel(S, 0, j, True)
                    if S.ada_iters and j == 2:
                        ada_sum(S.ada)
                if S.name == "ffn0_down":
                    ada_sum(15)
                cuts = [1, S.iters] if not 0 < S.ada_iters < S.iters else [1, S.ada_iters, S.iters]
                for a, b in zip(cuts, cuts[1:]):
                    if S.iters <= 2:
                        for j in range(len(S.panels)):
                            run_panel(S, 1, j, False)
                        continue
                    with pe.Fori(a, b) as i:
                        for j in range(len(S.panels)):
                            run_panel(S, i, j, False)
                            if a < S.ada_iters and j == 2:
                                ada_sum(i + S.ada)
            pe.wait_ge(ssq_added, KT * (len([s for s in UPDATES if s in RUN]) + 1) + 1)
            pe.matmul(stat_bank[:, 0:LAT], ones[:], ssq[:, 0:LAT], start=True, stop=True).then_inc(stat_done, 1)
            for n in range(4):
                c, half = n // 2, n % 2
                pe.wait_ge(f_normed, KT)
                for t in range(4):
                    mm = turn(ps[n][:, t * P:(t + 1) * P], y_out[:, 4 * half + t, c * P:(c + 1) * P])
                mm.then_inc(f_turned, 1)

        @block.scalar
        def _(act):
            act.sem_inc(conv_done, 2)
            act.sem_inc(s_ctx, 4)
            act.sem_inc(pt_act, 1)
            link = [0]

            def square(q, og, t, N):
                act.wait_ge(out_taken, og) if og is not None else act.wait_ge(x_taken, q + 1)
                act.wait_ge(ssq_added, q + 1)
                nc.scalar.activation(tmp[0][:, 0:N], trunk[:, ds(t, 1), 0:N].rearrange("p a b -> p (a b)"),
                                     ACT.Square).then_inc(square_done, 1)

            def root(n, N):
                act.wait_ge(var_done, n + 1)
                nc.scalar.activation(tmp[1][:, 0:N], tmp[0][:, 0:N], ACT.Sqrt).then_inc(root_done, 1)

            def norm(n, N, shift):
                if n:
                    root(n, N)
                for t in range(KT):
                    act.wait_ge(normed, KT * n + t + 1)
                    for v in range(N // LAT):
                        ins = nc.scalar.activation(h_hi[:, t, v * LAT:(v + 1) * LAT],
                                                   tmp[t % 2][:, v * LAT:(v + 1) * LAT], ACT.Identity,
                                                   bias=mods[:, shift + t, v:v + 1])
                    ins.then_inc(h_hi_done, 1)

            def tend(S, i, o):
                og = output(S, i, o)
                last = max(j for j in range(len(S.panels)) if S.panels[j][4] == o)
                N = S.tokens
                if S.kind == "up":
                    ug = i * 2 + (S.up0 + o)
                    act.wait_ge(panel_used, panel(S, i, last) + (1 + PAN))
                    act.wait_ge(out_taken, og + PAN)
                    nc.scalar.activation(tmp[0][:, 0:N], ps[S.bank0 + 2 * o][:, 0:N], ACT.Silu
                                         ).then_inc(silu_done, 1)
                    act.wait_ge(out_taken, og + (1 + PAN))
                    nc.scalar.activation(g_hi[:, ds(i * 2 + o, 1), 0:N].rearrange("p a b -> p (a b)"),
                                         tmp[1][:, 0:N], ACT.Copy).then_inc(g_hi_done, 1)
                elif S in UPDATES:
                    t = i * S.outs + o
                    square(t + KT * S.update, og + (1 + PAN), t, N)
                elif S.name == "xbc":
                    c = i * 4 + o
                    act.wait_ge(conv_step, c * CONV + CONV)
                    nc.scalar.activation(xbc[:, ds(c, 1), :].rearrange("p a b -> p (a b)"), tmp[o % 2][:], ACT.Silu
                                         ).then_inc(conv_done, 1)

            def pooled(n):
                act.wait_ge(pool_mm, n + 1)
                nc.scalar.activation(pooled_hi[:, n, :], ps[n][:], ACT.Copy,
                                     scale=vec[:, VEC["pool_scale"] + n:VEC["pool_scale"] + n + 1]
                                     ).then_inc(pool_hi, 1)

            def step(S, i, j, prior, first):
                if silu_first(S, j, first):
                    tend(*prior)
                    prior = None
                if S is not None:
                    slot, k0, nk, c0, _, _, _ = S.panels[j]
                    down = S.kind == "down"
                    group = i * S.groups + (S.group0 + j // PAN)
                    act.wait_ge(raw_loaded[slot], group * 16 + 16)
                    act.wait_ge(panel_used, panel(S, i, j) + 1)
                    src = raw[slot][:, 0:(11 * P if down else 16 * P)].rearrange("p (k m) -> p k m", k=11 if down else 8)
                    nc.scalar.activation(pan_hi[j % PAN][:, 0:nk, :], src[:, k0:k0 + nk, c0:c0 + P], ACT.Copy
                                         ).then_inc(hi_done, 1)
                if prior is not None:
                    tend(*prior)
                if first and j == LAG - 1:
                    after(RUN[S.index - 1].name if S is not None and S.index else "start" if S is not None else "end",
                          S)

            def after(name, S):
                if name == "xbc":
                    act.wait_ge(dt_abs, 1)
                    nc.scalar.activation(dt_b[:], dt_a[:], ACT.Exp, scale=-1.0).then_inc(dt_act, 1)
                    nc.scalar.activation(a_coef[:], vec[:, VEC["a_log"]:VEC["a_log"] + 32], ACT.Exp
                                         ).then_inc(dt_act, 1)
                if name == "z":
                    act.wait_ge(out_taken, BY["mix_out"].out0 + PAN)
                    nc.scalar.activation(zs[:], zs[:], ACT.Silu).then_inc(z_done, 1)
                    for n in range(4, 8):
                        pooled(n)
                    act.wait_ge(sums_mm, 1)
                    nc.scalar.activation(exps[:].rearrange("p a b c -> p (a b c)"), ps[4][:, 0:3 * P], ACT.Exp
                                         ).then_inc(exps_done, 1)
                    for u in range(len(UNITS)):
                        act.wait_ge(seg_mm, u + 1)
                        if u > 1:
                            act.wait_ge(weight_done, u - 1)
                        nc.scalar.activation(decay[u % 2][:].rearrange("p a b -> p (a b)"), ps[u % 2][:], ACT.Exp
                                             ).then_inc(decay_done, 1)
                    for t in range(KT):
                        act.wait_ge(y_gated, t + 1)
                        if t:
                            act.wait_ge(gn_added, t)
                        nc.scalar.activation(tmp[0][:], xbc[:, t, :], ACT.Square).then_inc(gn_square, 1)
                    act.wait_ge(gn_var, 1)
                    nc.scalar.activation(tmp[1][:], tmp[0][:], ACT.Sqrt).then_inc(gn_root, 1)
                    for t in range(KT):
                        act.wait_ge(y_gated, KT + t + 1)
                        nc.scalar.activation(y_hi[:, t, :], xbc[:, t, :], ACT.Copy).then_inc(y_hi_done, 1)
                if name == "q":
                    def soften(t, b, a):
                        for n in (2 * a, 2 * a + 1):
                            act.wait_ge(qk_mm, t * 4 + (n + 2))
                            act.wait_ge(pt_mm, t * 2 + (a + 1))
                            nc.scalar.activation(score[b][:, n, LAT:TOK], ps[n][:, LAT:TOK], ACT.Copy,
                                                 scale=HD ** -0.5).then_inc(s_ctx, 1)
                        for n in (2 * a, 2 * a + 1):
                            act.wait_ge(max_done, t * 4 + (n + 1))
                            nc.scalar.activation(score[b][:, n, :], score[b][:, n, :], ACT.Exp, bias=smax[:, n, 1:2],
                                                 accum_out=smax[:, n, 2:3]).then_inc(p_done, 1)

                    def pair(t, b, more):
                        for a in range(2):
                            act.wait_ge(pt_mm, t * 2 + (a + 5))
                            nc.scalar.activation(prob_t[a][:, 0:2, :].rearrange("p a b -> p (a b)"), ps[4][:], ACT.Copy
                                                 ).then_inc(pt_act, 1)
                            if more:
                                soften(t + 1, 1 - b, a)
                        act.wait_ge(pv_mm, t * 2 + 4)
                        nc.scalar.activation(o_hi[:, ds(t, 1), :].rearrange("p a b -> p (a b)"), ps[6][:, 0:LAT],
                                             ACT.Copy).then_inc(o_hi_done, 1)

                    soften(0, 0, 0)
                    soften(0, 0, 1)
                    head_pairs(act, pair)
                if S is not None and S.norm is not None:
                    norm(S.norm, S.tokens, (S.norm // 3) * 72 + 24 * (S.norm % 3))
                if name == "ffn0_down":
                    act.wait_ge(mixer_loaded, 48)
                    nc.scalar.activation(dt_hi[:], dt_raw[:], ACT.Copy).then_inc(dt_hi_done, 1)
                if name == "pool_in":
                    for n in range(4):
                        pooled(n)
                if name == "end":
                    root(len([s for s in UPDATES if s in RUN]), LAT)
                    for n in range(2):
                        act.wait_ge(f_turned, 2 * n + 2)
                        nc.scalar.activation(y_tok[:, n, 512:1024], ps[2 * n + 1][:], ACT.Copy
                                             ).then_inc(f_taken_act, 1)

            act.wait_ge(vec_loaded, 16)
            nc.scalar.activation(cond[:].rearrange("p a b -> p (a b)"), vec[:, 0:16], ACT.Silu).then_inc(cond_done, 1)
            for t in range(KT):
                square(t, None, t, TOK)
            root(0, TOK)
            walk(act, step)

        @block.vector
        def _(dve):
            link = [0]

            def chain(ins):
                link[0] += 1
                ins.then_inc(dve_link, 1)
                dve.wait_ge(dve_link, link[0])

            def tt(o, a, b, op):
                return nc.vector.tensor_tensor(o, a, b, op)

            nc.vector.memset(ones[:], 1.0).then_inc(ones_done, 1)
            dve.wait_ge(ones_done, 1)
            chain(nc.vector.memset(ssq[:], 0.0))
            dve.sem_inc(lo_done, PAN)
            dve.sem_inc(out_taken, PAN)
            dve.sem_inc(ssq_added, 1)
            dve.sem_inc(ada_step, 8 + 16 * ADA_FIRST)
            dve.sem_inc(g_ready, 1)
            dve.sem_inc(mods_done, 1)
            dve.sem_inc(s_done, 4)
            dve.sem_inc(pt_dve, 1)
            dve.sem_inc(o_done, 1)

            def add_square(q, N):
                dve.wait_ge(square_done, q + 1)
                dve.wait_ge(ssq_added, q + 1)
                tt(ssq[:, 0:N], ssq[:, 0:N], tmp[0][:, 0:N], ALU.add).then_inc(ssq_added, 1)

            def ada_quarter(b, q):
                dve.wait_ge(ada_loaded[q % 2], (b - ADA_FIRST) * 32 + ((q // 2) * 16 + 16))
                for kk in range(2):
                    for v in range(2):
                        n = 4 * q + 2 * kk + v
                        k = 2 * q + kk
                        dve.wait_ge(ada_step, b * 16 + (n - 2 + 1 + 8))
                        if n < 2:
                            ins = nc.vector.tensor_scalar(ada_acc[:, v, :], ada_raw[q % 2][:, kk, :],
                                                          cond[:, v, k:k + 1], None, ALU.mult)
                        else:
                            ins = nc.vector.scalar_tensor_tensor(out=ada_acc[:, v, :], in0=ada_raw[q % 2][:, kk, :],
                                                                 scalar=cond[:, v, k:k + 1], in1=ada_acc[:, v, :],
                                                                 op0=ALU.mult, op1=ALU.add)
                        ins.then_inc(ada_step, 1)

            def ada_take(b):
                dve.wait_ge(ada_summed, b + 1)
                tt(mods[:, ds(b * 4, 4), :], ada_bank[:, 0:8].rearrange("p (t v) -> p t v", v=2),
                   vec[:, ds(b * 4 + VEC["ada_b"], 4)][:, :, None].to_broadcast([P, 4, 2]), ALU.add
                   ).then_inc(mods_done, 1)

            def set_gate(l, chunk, factor):
                c0 = l * 72 + chunk * 8
                dve.wait_ge(mods_done, (c0 + 8) // 4 + 1)
                chain(nc.vector.tensor_scalar(gate[:], mods[:, c0:c0 + 8, :], factor, None, ALU.mult))

            def rstd(n, N, stat_sem, count, var_sem, root_sem):
                dve.wait_ge(stat_sem, count)
                nc.vector.tensor_scalar(tmp[0][:, 0:N], stat_bank[:, 0:N], 1.0 / D, EPS, ALU.mult, ALU.add
                                        ).then_inc(var_sem, 1)
                dve.wait_ge(root_sem, count)
                chain(nc.vector.reciprocal(ssq[:, 0:N], tmp[1][:, 0:N]))

            def norm(n, N):
                l, s = n // 3, n % 3
                sc = l * 72 + (3 * s + 1) * 8
                sh = l * 72 + 3 * s * 8
                V = N // LAT
                dve.wait_ge(mods_done, (sc + 8) // 4 + 1)
                g0 = VEC["norm_g"] + n * 8
                chain(nc.vector.scalar_tensor_tensor(out=norm_scale[:], in0=mods[:, sc:sc + 8, :], scalar=1.0,
                                                     in1=vec[:, g0:g0 + 8][:, :, None].to_broadcast([P, 8, 2]),
                                                     op0=ALU.add, op1=ALU.mult))
                if n:
                    rstd(n, N, stat_done, n + 1, var_done, root_done)

                def scaled(t):
                    if t > 1:
                        dve.wait_ge(h_ready, KT * n + t - 1)
                    for v in range(V):
                        sl = slice(v * LAT, (v + 1) * LAT)
                        ins = nc.vector.scalar_tensor_tensor(out=tmp[t % 2][:, sl], in0=trunk[:, t, sl],
                                                             scalar=norm_scale[:, t, v:v + 1], in1=ssq[:, sl],
                                                             op0=ALU.mult, op1=ALU.mult)
                    ins.then_inc(normed, 1)

                def low(t):
                    dve.wait_ge(h_hi_done, KT * n + t + 1)
                    for v in range(V):
                        sl = slice(v * LAT, (v + 1) * LAT)
                        ins = nc.vector.scalar_tensor_tensor(out=h_lo[:, t, sl], in0=tmp[t % 2][:, sl],
                                                             scalar=mods[:, sh + t, v:v + 1],
                                                             in1=h_hi[:, t, sl].bitcast(F32),
                                                             op0=ALU.add, op1=ALU.subtract)
                    ins.then_inc(h_ready, 1)

                scaled(0)
                for t in range(KT):
                    if t + 1 < KT:
                        scaled(t + 1)
                    low(t)
                chain(nc.vector.memset(ssq[:], 0.0))

            def update(S, i, o):
                og, t = output(S, i, o), i * S.outs + o
                b = ps[S.bank0 + o]
                for v in range(S.tokens // LAT):
                    sl = slice(v * LAT, (v + 1) * LAT)
                    x_t = trunk[:, ds(t, 1), sl].rearrange("p a b -> p (a b)")
                    ins = nc.vector.scalar_tensor_tensor(out=x_t, in0=b[:, sl],
                                                         scalar=gate[:, ds(t, 1), v:v + 1].rearrange("p a b -> p (a b)"),
                                                         in1=x_t, op0=ALU.mult, op1=ALU.add)
                ins.then_inc(out_taken, 1)
                add_square(t + KT * S.update, S.tokens)

            def conv(S, i, o):
                og, c = output(S, i, o), i * 4 + o
                pad, acc = conv_pad[o % 2], tmp[o % 2]
                acc3 = acc[:].rearrange("p (s t) -> p s t", s=2)
                dve.wait_ge(conv_done, c + 1)
                nc.vector.tensor_copy(pad[:, :, 2:2 + LAT], ps[S.bank0 + o][:].rearrange("p (s t) -> p s t", s=2)
                                      ).then_inc(out_taken, 1)
                dve.wait_ge(out_taken, og + (1 + PAN))
                for j in range(CONV):
                    w = vec[:, ds(c + (VEC["conv_w"] + j * NCONV), 1)]
                    if j == 0:
                        ins = nc.vector.tensor_scalar(acc3, pad[:, :, 0:LAT], w, vec[:, ds(c + VEC["conv_b"], 1)],
                                                      ALU.mult, ALU.add)
                    else:
                        dve.wait_ge(conv_step, c * CONV + j)
                        ins = nc.vector.scalar_tensor_tensor(out=acc3, in0=pad[:, :, j:j + LAT], scalar=w, in1=acc3,
                                                             op0=ALU.mult, op1=ALU.add)
                    ins.then_inc(conv_step, 1)

            def pool_tile(S, i, o):
                c = 4 * i + o
                g = c // 2
                w = WINDOWS[g]
                if c:
                    dve.wait_ge(mu_ready, c)
                nc.vector.tensor_copy(pool_u[:, :, PAD:PAD + LAT],
                                      ps[S.bank0 + o][:].rearrange("p (s t) -> p s t", s=2)).then_inc(out_taken, 1)
                dve.wait_ge(out_taken, output(S, i, o) + (1 + PAN))
                src, width, n = pool_u, 1, 0
                L = pw_len
                while width < w:
                    dst = pool_s[n % 2]
                    L -= width
                    chain(tt(dst[:, :, 0:L], src[:, :, 0:L], src[:, :, width:width + L], ALU.add))
                    src, width, n = dst, 2 * width, n + 1
                a = PAD - w // 2
                t3 = pool_s[n % 2]
                chain(tt(t3[:, :, 0:LAT], src[:, :, a:a + LAT],
                         inv_count[:, g, :][:, None, :].to_broadcast([P, 2, LAT]), ALU.mult))
                if g >= 2:
                    dve.wait_ge(pool_mm, 4)
                tt(mu[:, c % 4, :].rearrange("p (s t) -> p s t", s=2), t3[:, :, 0:LAT],
                   pool_u[:, :, PAD:PAD + LAT], ALU.subtract).then_inc(mu_ready, 1)

            def pooled(n):
                dve.wait_ge(pool_hi, n + 1)
                nc.vector.scalar_tensor_tensor(out=pooled_lo[:, n, :], in0=ps[n][:],
                                               scalar=vec[:, VEC["pool_scale"] + n:VEC["pool_scale"] + n + 1],
                                               in1=pooled_hi[:, n, :].bitcast(F32), op0=ALU.mult, op1=ALU.subtract
                                               ).then_inc(pool_lo, 1)

            def dt_steps():
                dve.wait_ge(dt_mm, 1)
                def over_chunks(a):
                    return a[:, None, :].to_broadcast([P, CHUNKS, 32])
                tt(dt_x[:], ps[7][:, 0:P].rearrange("p (c h) -> p c h", c=CHUNKS),
                   over_chunks(vec[:, VEC["dt_bias"]:VEC["dt_bias"] + 32]), ALU.add).then_inc(dt_taken, 1)
                dve.wait_ge(dt_taken, 1)

                def stt(o, a, s, b, op0, op1):
                    return nc.vector.scalar_tensor_tensor(out=o[:], in0=a[:], scalar=s, in1=b, op0=op0, op1=op1)

                stt(dt_a, dt_x, -1.0, dt_x[:], ALU.mult, ALU.max).then_inc(dt_abs, 1)
                dve.wait_ge(dt_act, 2)
                chain(nc.vector.tensor_scalar(dt_a[:], dt_b[:], 2.0, None, ALU.add))
                chain(nc.vector.reciprocal(dt_c[:], dt_a[:]))
                chain(tt(dt_a[:], dt_b[:], dt_c[:], ALU.mult))
                chain(tt(dt_b[:], dt_a[:], dt_a[:], ALU.mult))
                chain(nc.vector.tensor_scalar(dt_c[:], dt_b[:], 1.0 / 17, None, ALU.mult))
                for k in range(7, 0, -1):
                    chain(stt(dt_c, dt_c, 1.0 / (2 * k + 1), dt_b[:], ALU.add, ALU.mult))
                chain(stt(dt_c, dt_c, 1.0, dt_a[:], ALU.add, ALU.mult))
                chain(nc.vector.tensor_scalar(dt_c[:], dt_c[:], 2.0, None, ALU.mult))
                chain(stt(dt, dt_x, 0.0, dt_c[:], ALU.max, ALU.add))
                stt(dta, dt, -1.0, over_chunks(a_coef[:]), ALU.mult, ALU.mult).then_inc(dt_vec, 1)
                dve.wait_ge(dt_vec, 1)

            def ssd():
                def by_head(a, c, d, g):
                    return a[:, c, d * HEADS + 8 * g:d * HEADS + 8 * g + 8][:, :, None].to_broadcast([P, 8, HD])

                def heads(a):
                    return a.rearrange("p (h e) -> p h e", h=8)

                def over_heads(a):
                    return a[:, None, :].to_broadcast([P, 4, P])

                dve.wait_ge(tri_loaded, 16)

                def seg(u):
                    g, c, quad, d = UNITS[u]
                    if u > 1:
                        dve.wait_ge(seg_mm, u - 1)
                    h0 = d * HEADS + 8 * g + 4 * quad
                    tt(seg_rhs[u % 2][:], dta[:, c, h0:h0 + 4][:, :, None].to_broadcast([P, 4, P]),
                       over_heads(tri[:, d, :]), ALU.mult).then_inc(seg_ready, 1)

                for g in range(2):
                    for c in range(CHUNKS):
                        dve.wait_ge(xt_mm, CHUNKS * g + c + 1)
                        for d in range(2):
                            tt(heads(xd[d][:, c, :]), heads(ps[5 + c % 2][:]), by_head(dt, c, d, g), ALU.mult
                               ).then_inc(xd_done, 1)
                    dve.wait_ge(bt_mm, g + 1)
                    nc.vector.tensor_copy(b_tok[:].rearrange("p a b -> p (a b)"), ps[4][:]).then_inc(bt_done, 1)
                    dve.wait_ge(cb_mm, g + 1)
                    for d in range(2):
                        tt(cb[d][:], ps[7][:].rearrange("p (a b) -> p a b", a=CHUNKS), over_heads(tri[:, d, :]),
                           ALU.mult).then_inc(cb_done, 1)
                    dve.wait_ge(exps_done, 1)
                    dve.wait_ge(xd_done, 8 * (g + 1))

                    def decayed(n):
                        pos, d = n // 2, n % 2
                        c = ORDER[d][pos]
                        if n > 1:
                            dve.wait_ge(state_mm, 6 * g + n - 1)
                        tt(heads(xdd[n % 2][:]), heads(xd[d][:, c, :]), by_head(exps[:, 1], c, d, g), ALU.mult
                           ).then_inc(xdd_done, 1)

                    decayed(0)
                    for n in range(6):
                        pos, d = n // 2, n % 2
                        c = ORDER[d][pos]
                        if n < 5:
                            decayed(n + 1)
                        dve.wait_ge(state_mm, 6 * g + n + 1)
                        if pos == 0:
                            nc.vector.tensor_copy(states[d][:, 0, :], ps[5 + n % 2][:]).then_inc(state_done, 1)
                        else:
                            dve.wait_ge(state_done, 6 * g + n)
                            chain(tt(heads(tmp[1][:]), heads(states[d][:, pos - 1, :]), by_head(exps[:, 2], c, d, g),
                                     ALU.mult))
                            tt(states[d][:, pos, :], tmp[1][:], ps[5 + n % 2][:], ALU.add).then_inc(state_done, 1)
                    if g == 0:
                        seg(0)
                    for c in range(CHUNKS):
                        for n in range(4):
                            u = 16 * g + 4 * c + n
                            if u + 1 < len(UNITS):
                                seg(u + 1)
                            dve.wait_ge(decay_done, u + 1)
                            if u > 1:
                                dve.wait_ge(diag_mm, u - 1)
                            tt(weight[u % 2][:], decay[u % 2][:], over_heads(cb[n % 2][:, c, :]), ALU.mult
                               ).then_inc(weight_done, 1)
                        dve.wait_ge(off_mm, CHUNKS * g + c + 1)
                        if g or c:
                            dve.wait_ge(yt_mm, CHUNKS * g + c)
                        on = [d for d in range(2) if ORDER[d].index(c)]
                        for d in on:
                            chain(tt(heads(tmp[on.index(d)][:]), heads(ps[6 + d][:]), by_head(exps[:, 0], c, d, g),
                                     ALU.mult))
                        if len(on) > 1:
                            chain(tt(tmp[0][:], tmp[0][:], tmp[1][:], ALU.add))
                        dve.wait_ge(diag_mm, 16 * g + 4 * c + 4)
                        tt(tmp[0][:], tmp[0][:], ps[2 + c % 2][:], ALU.add).then_inc(y_sum, 1)
                        dve.wait_ge(yt_mm, CHUNKS * g + c + 1)
                        for t in range(4):
                            d0 = VEC["d_skip"] + 4 * g + t
                            x_t = xbc[:, 4 * g + t, c * P:(c + 1) * P]
                            ins = nc.vector.scalar_tensor_tensor(out=x_t, in0=x_t, scalar=vec[:, d0:d0 + 1],
                                                                 in1=ps[4][:, t * P:(t + 1) * P],
                                                                 op0=ALU.mult, op1=ALU.add)
                        ins.then_inc(yt_done, 1)
                dve.wait_ge(z_done, 1)
                dve.wait_ge(yt_done, 8)
                for t in range(KT):
                    tt(xbc[:, t, :], xbc[:, t, :], zs[:, t, :], ALU.mult).then_inc(y_gated, 1)
                for t in range(KT):
                    dve.wait_ge(gn_square, t + 1)
                    if t:
                        dve.wait_ge(gn_added, t)
                    tt(ssq[:], ssq[:], tmp[0][:], ALU.add).then_inc(gn_added, 1)
                rstd(0, TOK, gn_stat, 1, gn_var, gn_root)
                dve.wait_ge(y_gated, KT)

                def scaled(t):
                    g0 = VEC["gn_g"] + t
                    nc.vector.scalar_tensor_tensor(out=xbc[:, t, :], in0=xbc[:, t, :], scalar=vec[:, g0:g0 + 1],
                                                   in1=ssq[:], op0=ALU.mult, op1=ALU.mult).then_inc(y_gated, 1)

                scaled(0)
                for t in range(KT):
                    if t + 1 < KT:
                        scaled(t + 1)
                    dve.wait_ge(y_hi_done, t + 1)
                    tt(y_lo[:, t, :], xbc[:, t, :], y_hi[:, t, :].bitcast(F32), ALU.subtract).then_inc(y_ready, 1)
                chain(nc.vector.memset(ssq[:], 0.0))

            def attention():
                for t in range(KT):
                    dve.wait_ge(vt_mm, t + 1)
                    nc.vector.tensor_copy(v_tok[:, :, t * P:(t + 1) * P],
                                          ps[4 + t % 2][:].rearrange("p (c e) -> p c e", c=4)).then_inc(vt_done, 1)
                dve.wait_ge(masked, 2)

                def soften(t, b, a):
                    rows = (2 * a, 2 * a + 1)
                    for n in rows:
                        dve.wait_ge(s_ctx, t * 4 + (n + 5))
                        nc.vector.scalar_tensor_tensor(
                            out=score[b][:, n, 0:LAT].rearrange("p (r c) -> p r c", r=ROWS),
                            in0=ps[n][:, 0:LAT].rearrange("p (r c) -> p r c", r=ROWS), scalar=HD ** -0.5,
                            in1=bias[:, n % 2, ds(t * 2 + a, 1), :, :].rearrange("p h r c -> p (h r) c"),
                            op0=ALU.mult, op1=ALU.add).then_inc(s_done, 1)
                    for n in rows:
                        dve.wait_ge(s_done, t * 4 + (n + 5))
                        nc.vector.reduce_max(smax[:, n, 0:1], score[b][:, n, :], AX_X).then_inc(max_found, 1)
                        dve.wait_ge(max_found, t * 4 + (n + 1))
                        nc.vector.tensor_scalar(smax[:, n, 1:2], smax[:, n, 0:1], -1.0, None, ALU.mult
                                                ).then_inc(max_done, 1)
                    for n in rows:
                        dve.wait_ge(p_done, t * 4 + (n + 1))
                        nc.vector.reciprocal(smax[:, n, 3:4], smax[:, n, 2:3]).then_inc(sum_inverted, 1)
                        dve.wait_ge(sum_inverted, t * 4 + (n + 1))
                        nc.vector.tensor_scalar(score[b][:, n, :], score[b][:, n, :], smax[:, n, 3:4], None, ALU.mult
                                                ).then_inc(p_norm, 1)

                def pair(t, b, more):
                    for a in range(2):
                        dve.wait_ge(pt_mm, t * 2 + (a + 5))
                        nc.vector.tensor_copy(prob_t[a][:, 2:4, :].rearrange("p a b -> p (a b)"), ps[5][:]
                                              ).then_inc(pt_dve, 1)
                        if more:
                            soften(t + 1, 1 - b, a)
                    dve.wait_ge(pv_mm, t * 2 + 4)
                    dve.wait_ge(o_hi_done, t + 1)
                    tt(o_lo[:, ds(t, 1), :].rearrange("p a b -> p (a b)"), ps[6][:, 0:LAT],
                       o_hi[:, ds(t, 1), :].bitcast(F32).rearrange("p a b -> p (a b)"), ALU.subtract
                       ).then_inc(o_done, 1)

                soften(0, 0, 0)
                soften(0, 0, 1)
                head_pairs(dve, pair)

            def tend(S, i, o):
                og = output(S, i, o)
                last = max(j for j in range(len(S.panels)) if S.panels[j][4] == o)
                if S.kind == "up":
                    ug = i * 2 + (S.up0 + o)
                    N = S.tokens
                    dve.wait_ge(panel_used, panel(S, i, last) + (1 + PAN))
                    dve.wait_ge(silu_done, ug + 1)
                    dve.wait_ge(g_ready, ug + 1)
                    tt(tmp[1][:, 0:N], tmp[0][:, 0:N], ps[S.bank0 + 2 * o + 1][:, 0:N], ALU.mult
                       ).then_inc(out_taken, 1)

                    dve.wait_ge(g_hi_done, ug + 1)
                    g_t = ds(i * 2 + o, 1)
                    tt(g_lo[:, g_t, 0:N].rearrange("p a b -> p (a b)"), tmp[1][:, 0:N],
                       g_hi[:, g_t, 0:N].bitcast(F32).rearrange("p a b -> p (a b)"), ALU.subtract
                       ).then_inc(g_ready, 1)
                    return
                dve.wait_ge(panel_used, panel(S, i, last) + (1 + PAN))
                if S in UPDATES:
                    update(S, i, o)
                elif S.name == "xbc":
                    conv(S, i, o)
                elif S.name == "pool_in":
                    pool_tile(S, i, o)
                else:
                    dst = {"z": zs, "k": kt_all, "v": vt_all, "q": qt_all}[S.name]
                    N = S.tokens
                    nc.vector.tensor_copy(dst[:, 4 * i + o, 0:N], ps[S.bank0 + o][:, 0:N]).then_inc(out_taken, 1)

            def step(S, i, j, prior, first):
                if silu_first(S, j, first):
                    tend(*prior)
                    prior = None
                if S is not None:
                    slot, k0, nk, c0, _, _, _ = S.panels[j]
                    down = S.kind == "down"
                    dve.wait_ge(hi_done, panel(S, i, j) + 1)
                    src = raw[slot][:, 0:(11 * P if down else 16 * P)].rearrange("p (k m) -> p k m", k=11 if down else 8)
                    tt(pan_lo[j % PAN][:, 0:nk, :], src[:, k0:k0 + nk, c0:c0 + P],
                       pan_hi[j % PAN][:, 0:nk, :].bitcast(F32), ALU.subtract).then_inc(lo_done, 1)
                ada = S is not None and S.ada_iters and (i < S.ada_iters if isinstance(i, int) else
                                                         S.at < S.ada_iters)
                pend = S is not None and S.ada_iters and not first and (i <= S.ada_iters if isinstance(i, int)
                                                                        else S.at <= S.ada_iters)
                if pend and j == 1:
                    ada_take(i + (S.ada - 1))
                if ada and not first and j >= 1:
                    ada_quarter(i + S.ada, j - 1)
                B = RUN[S.index - 1] if S is not None and S.index and first and j == 0 else None
                if pend and j == 0:
                    ada_quarter(i + (S.ada - 1), 3)
                elif B and B.ada_iters == B.iters:
                    ada_quarter(B.ada + B.iters - 1, 3)
                if prior is not None:
                    tend(*prior)
                if first and j == LAG - 1:
                    after(RUN[S.index - 1].name if S is not None and S.index else "start" if S is not None else "end",
                          S)
                if ada and first and j == 3:
                    for q in range(3):
                        ada_quarter(i + S.ada, q)

            def after(name, S):
                if name.endswith("_up"):
                    A = BY[name]
                    if A.ada_iters == A.iters:
                        ada_take(A.ada + A.iters - 1)
                    l, half = A.arg
                    if name == "ffn0_up":
                        for q in range(4):
                            ada_quarter(15, q)
                    set_gate(l, 2 if half == 0 else 8, 0.5)
                if name == "ffn0_down":
                    ada_take(15)
                if name == "xbc":
                    dt_steps()
                    chain(nc.vector.memset(pool_u[:], 0.0))
                if name == "pool_in":
                    for n in range(4):
                        pooled(n)
                if name == "z":
                    for n in range(4, 8):
                        pooled(n)
                    ssd()
                    set_gate(0, 5, 1.0)
                if name in ("k", "v"):
                    half = int(name == "v")
                    dve.wait_ge(bias_loaded, 128 * (half + 1))
                    dve.wait_ge(mask_loaded, 16)
                    tt(bias[:, half, :, :, :].rearrange("p h r c -> p (h r) c"),
                       bias_rev[:, :, :, ::-1].rearrange("p h r c -> p (h r) c"),
                       na_mask[:, None, :].to_broadcast([P, HEADS * ROWS, GRID_W]), ALU.add).then_inc(masked, 1)
                if name == "q":
                    attention()
                    set_gate(1, 5, 1.0)
                if S is not None and S.norm is not None:
                    norm(S.norm, S.tokens)
                if name == "ffn0_down":
                    for pad in conv_pad:
                        chain(nc.vector.memset(pad[:], 0.0))
                    dve.wait_ge(dt_hi_done, 1)
                    tt(dt_lo[:], dt_raw[:], dt_hi[:].bitcast(F32), ALU.subtract).then_inc(dt_split, 1)
                if name == "end":
                    n = len([s for s in UPDATES if s in RUN])
                    rstd(n, LAT, stat_done, n + 1, var_done, root_done)
                    for t in range(KT):
                        g0 = VEC["final_g"] + t
                        nc.vector.scalar_tensor_tensor(out=y_out[:, t, :], in0=trunk[:, t, 0:LAT],
                                                       scalar=vec[:, g0:g0 + 1], in1=ssq[:, 0:LAT],
                                                       op0=ALU.mult, op1=ALU.mult).then_inc(f_normed, 1)
                    for n in range(2):
                        dve.wait_ge(f_turned, 2 * n + 1)
                        nc.vector.tensor_copy(y_tok[:, n, 0:512], ps[2 * n][:]).then_inc(f_taken_dve, 1)

            for t in range(KT):
                dve.wait_ge(x_turned, t + 1)
                nc.vector.tensor_copy(trunk[:, t, :], ps[t % 2][:]).then_inc(x_taken, 1)
                add_square(t, TOK)
            rstd(0, TOK, stat_done, 1, var_done, root_done)
            for b in range(ADA_FIRST):
                dve.wait_ge(rows_mm, b + 1)
                nc.vector.tensor_copy(ada_rows[:, b, :], ps[2 + b][0:2, :]).then_inc(rows_taken, 1)
            dve.wait_ge(rows_turned, 1)
            nt = ADA_FIRST * 4
            tt(mods[:, 0:nt, :], ada_bank[:, 0:2 * nt].rearrange("p (t v) -> p t v", v=2),
               vec[:, VEC["ada_b"]:VEC["ada_b"] + nt][:, :, None].to_broadcast([P, nt, 2]), ALU.add
               ).then_inc(mods_done, ADA_FIRST)
            walk(dve, step)


def kernel(x, c, ctx, c_ctx, ada_w, ada_b, norm_g, ffn_w1, ffn_w3, ffn_w2, ssd_in_w, ssd_conv_w, ssd_conv_b,
           ssd_dt_bias, ssd_a_log, ssd_d, ssd_norm_g, pool_w, pool_scale, mix_a_out_w, na_qkv_w, na_rpb, na_out_w,
           final_norm_g):
    import concourse.bacc as bacc
    from concourse.bass_utils import run_bass_kernel_spmd

    def columns(a):
        return np.asarray(a).reshape(-1, P).T

    rows = {"c": columns(c), "c_ctx": columns(c_ctx), "norm_g": columns(norm_g), "ada_b": columns(ada_b),
            "conv_b": columns(ssd_conv_b), "conv_w": columns(ssd_conv_w), "gn_g": columns(ssd_norm_g),
            "pool_scale": columns(pool_scale), "d_skip": columns(np.repeat(np.asarray(ssd_d), HD)),
            "final_g": columns(final_norm_g),
            "dt_bias": np.broadcast_to(np.asarray(ssd_dt_bias).reshape(1, 32), (P, 32)),
            "a_log": np.broadcast_to(np.asarray(ssd_a_log).reshape(1, 32), (P, 32))}
    packed = np.ascontiguousarray(np.concatenate([rows[n] for n, _ in VEC_SIZES], axis=1))

    i, j = np.arange(P)[:, None], np.arange(P)[None, :]
    q, k = np.arange(P)[:, None] % GRID_W, np.arange(GRID_W)[None, :]
    start = np.clip(q - WIN_C // 2, 0, GRID_W - WIN_C)
    mask = np.where((k >= start) & (k < start + WIN_C), 0.0, NEG)
    consts = np.concatenate([i == j, mask, i <= j, i >= j, i > j, i < j], axis=1).astype(np.float32)
    t, w = np.arange(LAT)[None, :], np.array(WINDOWS)[:, None]
    lo, hi = np.clip(t - w // 2, 0, LAT - 1), np.clip(t + w - 1 - w // 2, 0, LAT - 1)
    inverse = (1.0 / (hi - lo + 1)).astype(np.float32).reshape(1, -1)
    inverse = np.ascontiguousarray(np.broadcast_to(inverse, (P, inverse.shape[1])))

    arrays = {"in_x": x, "in_ctx": ctx, "in_vec": packed, "in_const": consts, "in_inv": inverse, "in_ada_w": ada_w,
              "in_w1": ffn_w1, "in_w3": ffn_w3, "in_w2": ffn_w2, "in_in_w": ssd_in_w, "in_pool_w": pool_w,
              "in_mix_w": mix_a_out_w, "in_qkv_w": na_qkv_w, "in_rpb": np.asarray(na_rpb)[..., ::-1], "in_na_w": na_out_w}
    arrays = {n: np.ascontiguousarray(a) for n, a in arrays.items()}
    nc = bacc.Bacc("TRN2", target_bir_lowering=False, num_devices=1)
    args = [nc.dram_tensor(n, a.shape, mybir.dt.from_np(a.dtype), kind="ExternalInput").ap()
            for n, a in arrays.items()]
    args.append(nc.dram_tensor("out_0", (1, LAT, D), F32, kind="ExternalOutput").ap())
    build(nc, *args)
    r = run_bass_kernel_spmd(nc, [arrays], core_ids=[0])
    return r.results[0]["out_0"]
```

```python
from contextlib import ExitStack

import concourse.bass as bass
import concourse.mybir as mybir
from concourse.alu_op_type import AluOpType as ALU
import numpy as np

F32, F32R = mybir.dt.float32, mybir.dt.float32r
ACT = mybir.ActivationFunctionType
AX_X = mybir.AxisListType.X
ds = bass.ds

P = 128
D = 1024
KT = D // P
LAT, CTX = 256, 256
TOK = LAT + CTX
FF = 2816
FT = FF // P
HALF_FF = FF // 2
NMOD = 9
EPS = 1e-6
PAN = 4
LAG = 3
PANEL = 8 * P
HEADS = 16
HD = 64
GROUP_HEADS = 8
CHUNKS = TOK // P
CONV = 5
TAPS = CONV - 1
WINDOWS = (2, 4, 8, 16)
PAD = 8
NCONV = 12
ADA_COLS = 512
ADA_BLOCKS = NMOD * D // ADA_COLS
ADA_FIRST = 2 * D // ADA_COLS
GRID_W, WIN_C, ROWS = 64, 16, 4
RPB_R, RPB_C = 15, 31
NEG = -1.0e30

VEC_SIZES = [("c", 8), ("c_ctx", 8), ("norm_g", 48), ("ada_b", 144), ("conv_b", 12), ("conv_w", 60), ("gn_g", 8),
             ("pool_scale", 8), ("d_skip", 8), ("final_g", 8), ("dt_bias", 32), ("a_log", 32)]
VEC, _at = {}, 0
for _n, _s in VEC_SIZES:
    VEC[_n] = _at
    _at += _s
NVEC = _at


class Stage:

    def __init__(self, name, kind, iters, tokens=TOK, norm=None, arg=None, ada=None):
        self.name, self.kind, self.iters, self.tokens, self.norm, self.arg = name, kind, iters, tokens, norm, arg
        self.ada = ada
        if kind == "up":
            self.panels = [(0, 0, 8, 0, 0, 0, 0), (1, 0, 8, 0, 0, 1, 0), (0, 0, 8, P, 1, 0, 0), (1, 0, 8, P, 1, 1, 0)]
            self.outs = 2
        elif kind == "down":
            self.panels = [(s, k, n, 0, o, 0, 11 * s + k) for o in range(2) for s in range(2)
                           for k, n in ((0, 6), (6, 5))]
            self.outs = 2
        elif kind == "mix":
            self.panels = [(s, 0, 8, P * o, o, 0, 8 * s) for s in (1, 0) for o in range(2)]
            self.outs = 2
        else:
            self.panels = [(o // 2, 0, 8, P * (o % 2), o, 0, 0) for o in range(4)]
            self.outs = 4
        self.groups = len(self.panels) // PAN

    def opens(self, j):
        return self.panels[j][4:6] not in [p[4:6] for p in self.panels[:j]]

    def closes(self, j):
        o = self.panels[j][4]
        return o if o not in [p[4] for p in self.panels[j + 1:]] else None

    def slab_ends(self, slot):
        return max(j for j in range(PAN) if self.panels[j][0] == slot)


STAGES = [
    Stage("ffn0_up", "up", 11, norm=0, arg=(0, 0), ada=ADA_FIRST), Stage("ffn0_down", "down", 4, arg=(0, 0)),
    Stage("xbc", "lin", 3, norm=1, arg=1024), Stage("pool_in", "lin", 2, arg=2592), Stage("z", "lin", 2, arg=0),
    Stage("mix_out", "mix", 4),
    Stage("ffn1_up", "up", 11, norm=2, arg=(0, 1), ada=16), Stage("ffn1_down", "down", 4, arg=(0, 1)),
    Stage("ffn2_up", "up", 11, norm=3, arg=(1, 0), ada=26), Stage("ffn2_down", "down", 4, arg=(1, 0)),
    Stage("k", "lin", 2, norm=4, arg=1024), Stage("v", "lin", 2, arg=2048), Stage("q", "lin", 2, tokens=LAT, arg=0),
    Stage("na_out", "lin", 2, tokens=LAT, arg=0),
    Stage("ffn3_up", "up", 11, tokens=LAT, norm=5, arg=(1, 1)), Stage("ffn3_down", "down", 4, tokens=LAT, arg=(1, 1)),
]
RUN = STAGES
_p = _o = _g = _u = 0
for _i, _s in enumerate(STAGES):
    _s.index, _s.panel0, _s.out0, _s.group0, _s.up0 = _i, _p, _o, _g, _u
    _s.bank0 = 4 * (_i % 2)
    _p += len(_s.panels) * _s.iters
    _o += _s.outs * _s.iters
    _g += _s.groups * _s.iters
    _u += _s.outs * _s.iters if _s.kind == "up" else 0
BY = {s.name: s for s in STAGES}
UPDATES = [s for s in STAGES if s.kind in ("down", "mix") or s.name == "na_out"]
for _i, _s in enumerate(UPDATES):
    _s.update = _i + 1
FWD_ORDER, BWD_ORDER = (2, 3, 0, 1), (3, 2, 1, 0)
ORDER = (FWD_ORDER, BWD_ORDER)
UNITS = [(g, c, quad, d) for g in range(2) for c in range(CHUNKS) for quad in range(2) for d in range(2)]


def build(nc, x, ctx_in, vec_in, const_in, inv_in, ada_w, w1, w3, w2, in_w, pool_w, mix_w, qkv_w, rpb, na_w, out):
    ctx = ExitStack()
    with ctx:
        base = [16512]

        def at(name, shape, dt=F32, offset=None):
            size = 4
            for s in shape[1:]:
                size *= s
            if offset is None:
                offset = base[0]
                base[0] += size
            return nc.alloc_sbuf_tensor_at(name, shape, dt, offset=offset)

        def sem(name):
            return ctx.enter_context(nc.semaphore(name))

        trunk = at("trunk", [P, KT, TOK])
        h_at = base[0]
        h_hi = at("h_hi", [P, KT, TOK], F32R)
        h_lo = at("h_lo", [P, KT, TOK], F32R)
        h_mid = at("h_mid", [P, KT, TOK], offset=h_at + KT * TOK * 4)
        g_at = base[0]
        g_hi = at("g_hi", [P, FT, TOK], F32R)
        g_lo = at("g_lo", [P, FT, TOK], F32R)
        raw = [at(f"raw{i}", [P, 2048]) for i in range(2)]
        ada_at = base[0]
        ada_raw = [at(f"ada_raw{i}", [P, 2, ADA_COLS]) for i in range(2)]
        pan_hi = [at(f"pan_hi{i}", [P, 8, P], F32R) for i in range(PAN)]
        pan_lo = [at(f"pan_lo{i}", [P, 8, P], F32R) for i in range(PAN)]
        acc_at = base[0]
        ada_acc = at("ada_acc", [P, 2, ADA_COLS])
        vec = at("vec", [P, NVEC])
        mods = at("mods", [P, 2 * NMOD * KT, 2])
        norm_scale = at("norm_scale", [P, KT, 2])
        gate = at("gate", [P, KT, 2])
        cond = at("cond", [P, 2, KT])
        ident = at("ident", [P, P])
        na_mask = at("na_mask", [P, GRID_W])
        ones = at("ones", [P, P])
        tmp = [at(f"tmp{i}", [P, TOK]) for i in range(2)]
        ssq = at("ssq", [P, TOK])
        eps_end = base[0]
        assert eps_end <= 229344, eps_end

        f = 4
        x_in = at("x_in", [P, 4, D], offset=g_at)
        ada_first = at("ada_first", [P, ADA_FIRST, KT, ADA_COLS], offset=g_at + 4096 * f)
        ada_rows = at("ada_rows", [2, ADA_FIRST, ADA_COLS], offset=g_at + 20480 * f)
        pooled_hi = at("pooled_hi", [P, KT, TOK], F32R, offset=g_at)
        pooled_lo = at("pooled_lo", [P, KT, TOK], F32R, offset=g_at + 4096 * f)
        xbc = at("xbc", [P, NCONV, TOK], offset=g_at + 8192 * f)
        zs_at = g_at + 14336 * f
        zs = at("zs", [P, KT, TOK], offset=zs_at)
        conv_pad = [at(f"conv_pad{i}", [P, 2, LAT + 4], offset=zs_at + i * 520 * f) for i in range(2)]
        pw_len = LAT + 2 * PAD
        pool_u = [at(f"pool_u{i}", [P, 2, pw_len], offset=zs_at + 3456 * i * f) for i in range(2)]
        pool_s = [at(f"pool_s{i}", [P, 2, pw_len], offset=zs_at + (i + 1) * 2 * pw_len * f) for i in range(2)]
        inv_count = at("inv_count", [P, 4, LAT], offset=zs_at + 1664 * f)
        dt_raw = at("dt_raw", [P, KT, 32], offset=zs_at + 2688 * f)
        dt_hi = at("dt_hi", [P, KT, 32], F32R, offset=zs_at + 2944 * f)
        dt_lo = at("dt_lo", [P, KT, 32], F32R, offset=zs_at + 3200 * f)
        st_at = g_at + 18432 * f
        pool_wt = at("pool_wt", [P, 4, 2, 2 * P], offset=st_at)
        mu = [at(f"mu{i}", [P, 4, TOK], offset=(st_at + 2048 * f, g_at + 6144 * f)[i]) for i in range(2)]
        b_tok = at("b_tok", [P, CHUNKS, P], offset=st_at)
        states = [at(f"state{d}", [P, 3, 512], offset=st_at + (512 + d * 1536) * f) for d in range(2)]
        xd = [at(f"xd{d}", [P, CHUNKS, 512], offset=h_at + d * 2048 * f) for d in range(2)]
        seg_rhs = [at(f"seg_rhs{i}", [P, 4, P], offset=h_at + (4096 + 512 * i) * f) for i in range(2)]
        decay = [at(f"decay{i}", [P, 4, P], offset=h_at + (5120 + 512 * i) * f) for i in range(2)]
        weight = [at(f"weight{i}", [P, 4, P], offset=h_at + (6144 + 512 * i) * f) for i in range(2)]
        xdd = [at(f"xdd{i}", [P, 512], offset=h_at + (7168 + 512 * i) * f) for i in range(2)]
        y_sq = at("y_sq", [P, 4, P], offset=st_at + 3584 * f)
        y_hi = at("y_hi", [P, KT, TOK], F32R, offset=h_at)
        y_lo = at("y_lo", [P, KT, TOK], F32R, offset=h_at + 4096 * f)
        tri = at("tri", [P, 4, P], offset=ada_at)
        cb = [at(f"cb{d}", [P, CHUNKS, P], offset=ada_at + (512 + 512 * d) * f) for d in range(2)]
        exps = at("exps", [P, 3, CHUNKS, 32], offset=ada_at + 1536 * f)
        dt_x = at("dt_x", [P, CHUNKS, 32], offset=acc_at)
        dt_a = at("dt_a", [P, CHUNKS, 32], offset=acc_at + 128 * f)
        dt_b = at("dt_b", [P, CHUNKS, 32], offset=acc_at + 256 * f)
        dt_c = at("dt_c", [P, CHUNKS, 32], offset=acc_at + 384 * f)
        dt = at("dt", [P, CHUNKS, 32], offset=acc_at + 512 * f)
        dta = at("dta", [P, CHUNKS, 32], offset=acc_at + 640 * f)
        a_coef = at("a_coef", [P, 32], offset=acc_at + 768 * f)
        kt_all = at("kt_all", [P, KT, TOK], offset=g_at)
        vt_all = at("vt_all", [P, KT, TOK], offset=g_at + 4096 * f)
        o_hi = at("o_hi", [P, KT, LAT], F32R, offset=g_at + 4096 * f)
        o_lo = at("o_lo", [P, KT, LAT], F32R, offset=g_at + 6144 * f)
        qt_all = at("qt_all", [P, KT, LAT], offset=g_at + 8192 * f)
        v_tok = at("v_tok", [P, 4, D], offset=g_at + 10240 * f)
        bias_rev = at("bias_rev", [P, HEADS, ROWS, GRID_W], offset=g_at + 10240 * f)
        bias = at("bias", [P, 2, HEADS, ROWS, GRID_W], offset=g_at + 14336 * f)
        q_s = [at(f"q_s{i}", [P, LAT], offset=h_at + 256 * i * f) for i in range(2)]
        k_s = [at(f"k_s{i}", [P, TOK], offset=h_at + (512 + 512 * i) * f) for i in range(2)]
        v_s = at("v_s", [P, 4, P], offset=h_at + 1536 * f)
        score = [at(f"score{i}", [P, 4, TOK], offset=h_at + (2048 + 2048 * i) * f) for i in range(2)]
        prob_t = [at(f"prob_t{i}", [P, 4, LAT], offset=h_at + (6144 + 1024 * i) * f) for i in range(2)]
        smax = at("smax", [P, 4, 4], offset=acc_at)
        y_out = at("y_out", [P, KT, LAT], offset=g_at)
        y_tok = at("y_tok", [P, 2, D], offset=g_at + 2048 * f)

        ps = [ctx.enter_context(nc.psum_tensor(f"bank{i}", [P, 512], F32)) for i in range(8)]
        ada_bank, stat_bank = ps[6], ps[7]

        vec_loaded, const_loaded, x_loaded, mask_loaded = (sem(n) for n in ("vec_loaded", "const_loaded", "x_loaded",
                                                                           "mask_loaded"))
        raw_loaded = [sem(f"raw_loaded{i}") for i in range(2)]
        ada_loaded = [sem(f"ada_loaded{i}") for i in range(2)]
        mixer_loaded, tri_loaded = sem("mixer_loaded"), sem("tri_loaded")
        bias_loaded = sem("bias_loaded")
        hi_done, lo_done = sem("hi_done"), sem("lo_done")
        panel_used = sem("panel_used")
        out_taken = sem("out_taken")
        silu_done, g_hi_done, g_ready = sem("silu_done"), sem("g_hi_done"), sem("g_ready")
        square_done, ssq_added = sem("square_done"), sem("ssq_added")
        stat_done, var_done, root_done = sem("stat_done"), sem("var_done"), sem("root_done")
        normed, h_hi_done, h_ready = sem("normed"), sem("h_hi_done"), sem("h_ready")
        ada_step, ada_summed, mods_done = sem("ada_step"), sem("ada_summed"), sem("mods_done")
        cond_done, ones_done = sem("cond_done"), sem("ones_done")
        x_turned, x_taken = sem("x_turned"), sem("x_taken")
        first_loaded = [sem(f"first_loaded{b}") for b in range(ADA_FIRST)]
        rows_mm, rows_taken, rows_turned = sem("rows_mm"), sem("rows_taken"), sem("rows_turned")
        dve_link = sem("dve_link")
        act_link = sem("act_link")
        conv_first, conv_step, conv_done = (sem(n) for n in ("conv_first", "conv_step", "conv_done"))
        dt_split, dt_mm, dt_taken, dt_act, dt_vec = (sem(n) for n in ("dt_split", "dt_mm", "dt_taken", "dt_act",
                                                                      "dt_vec"))
        pool_in_taken, pool_link = sem("pool_in_taken"), sem("pool_link")
        mu_ready, pool_mm, pool_hi, pool_lo = sem("mu_ready"), sem("pool_mm"), sem("pool_hi"), sem("pool_lo")
        z_done = sem("z_done")
        dt_abs, dt_hi_done = sem("dt_abs"), sem("dt_hi_done")
        sums_mm, exps_done = sem("sums_mm"), sem("exps_done")
        xt_mm, xd_done, bt_mm, bt_done, cb_mm, cb_done = (sem(n) for n in ("xt_mm", "xd_done", "bt_mm", "bt_done",
                                                                          "cb_mm", "cb_done"))
        xdd_done, state_mm, state_done = sem("xdd_done"), sem("state_mm"), sem("state_done")
        seg_ready, seg_mm, decay_done, weight_done, diag_mm = (sem(n) for n in ("seg_ready", "seg_mm", "decay_done",
                                                                               "weight_done", "diag_mm"))
        off_mm, y_sum, yt_mm, yt_done = sem("off_mm"), sem("y_sum"), sem("yt_mm"), sem("yt_done")
        y_gated, y_hi_done, y_ready = sem("y_gated"), sem("y_hi_done"), sem("y_ready")
        gn_square, gn_added, gn_stat, gn_var, gn_root = (sem(n) for n in ("gn_square", "gn_added", "gn_stat",
                                                                         "gn_var", "gn_root"))
        vt_mm, vt_done = sem("vt_mm"), sem("vt_done")
        masked, q_staged, v_staged, qk_mm = sem("masked"), sem("q_staged"), sem("v_staged"), sem("qk_mm")
        s_ctx, s_done, p_done, p_norm = sem("s_ctx"), sem("s_done"), sem("p_done"), sem("p_norm")
        pt_mm, pt_act, pt_dve, pv_mm, o_hi_done, o_done = (sem(n) for n in ("pt_mm", "pt_act", "pt_dve", "pv_mm",
                                                                           "o_hi_done", "o_done"))
        max_done, max_found, sum_inverted = sem("max_done"), sem("max_found"), sem("sum_inverted")
        f_normed, f_turned, stored = sem("f_normed"), sem("f_turned"), sem("stored")
        f_taken_dve, f_taken_act = sem("f_taken_dve"), sem("f_taken_act")

        block = ctx.enter_context(nc.Block())

        def panel(S, i, j):
            return i * len(S.panels) + (S.panel0 + j)

        def output(S, i, o):
            return i * S.outs + (S.out0 + o)

        def bank(S, j):
            p = S.panels[j]
            return ps[S.bank0 + (2 * p[4] + p[5] if S.kind == "up" else p[4])]

        def halves(n):
            both = BY["ffn3_up"].norm
            return n + min(n, both)

        def walk(eng, step):
            def iteration(S, i, first):
                for j in range(len(S.panels)):
                    q = j - LAG
                    if q >= 0:
                        R, ri = S, i
                    elif not first:
                        R, ri, q = S, i - 1, len(S.panels) + q
                    else:
                        R = RUN[S.index - 1] if S.index else None
                        ri, q = (R.iters - 1, len(R.panels) + q) if R else (0, 0)
                    o = R.closes(q) if R else None
                    step(S, i, j, (R, ri, o) if o is not None else None, first)

            for S in RUN:
                iteration(S, 0, True)
                cuts = [1, 2, S.iters] if S.ada or S.name == "ffn0_down" else [1, S.iters]
                for a, b in zip(cuts, cuts[1:]):
                    if b - a <= 1:
                        for i in range(a, b):
                            iteration(S, i, False)
                    else:
                        with eng.Fori(a, b) as i:
                            iteration(S, i, False)
            last = RUN[-1]
            for q in range(LAG):
                o = last.closes(len(last.panels) - LAG + q)
                step(None, 0, q, (last, last.iters - 1, o) if o is not None else None, True)

        def head_pairs(eng, step):
            with eng.Fori(0, KT // 2 - 1) as m:
                for b in range(2):
                    step(m * 2 + b, b, True)
            step(KT - 2, 0, True)
            step(KT - 1, 1, False)

        def normed_stage(S):
            return S is not None and S.norm is not None

        def silu_first(S, j, first):
            return S is not None and S.kind == "up" and S.tokens == LAT and j == 0 and not first

        @block.sync
        def _(sp):
            sp.dma_start(vec[:], vec_in).then_inc(vec_loaded, 16)
            sp.dma_start(x_in[:, 0:2, :], x.rearrange("b (c p) d -> p (b c) d", p=P)).then_inc(x_loaded, 16)
            sp.dma_start(x_in[:, 2:4, :], ctx_in.rearrange("b (c p) d -> p (b c) d", p=P)).then_inc(x_loaded, 16)
            sp.dma_start(ident[:], const_in[:, 0:P]).then_inc(const_loaded, 16)
            for b in range(ADA_FIRST):
                src = ada_w[0][:, b * ADA_COLS:(b + 1) * ADA_COLS]
                sp.dma_start(ada_first[:, b], src.rearrange("(k p) m -> p k m", p=P)).then_inc(first_loaded[b], 16)
            sp.dma_start(na_mask[:], const_in[:, P:P + GRID_W]).then_inc(mask_loaded, 16)

            def slab(S, i, group, s):
                if S.kind == "up":
                    w = (w1, w3)[s][S.arg[0], S.arg[1]]
                    src = w[:, ds(i * 2 * P, 2 * P)].rearrange("(k p) m -> p k m", p=P)
                elif S.kind == "down":
                    w = w2[S.arg[0], S.arg[1]]
                    src = w[s * HALF_FF:(s + 1) * HALF_FF, ds(i * 2 * P + group * P, P)]
                    src = src.rearrange("(k p) m -> p k m", p=P)
                elif S.kind == "mix":
                    src = mix_w[0][s * D:(s + 1) * D, ds(i * 2 * P, 2 * P)].rearrange("(k p) m -> p k m", p=P)
                else:
                    w = in_w[0] if S.name in ("xbc", "pool_in", "z") else na_w[0] if S.name == "na_out" else qkv_w[0]
                    src = w[:, ds(i * 4 * P + (S.arg + s * 2 * P), 2 * P)].rearrange("(k p) m -> p k m", p=P)
                return src

            def group_loads(S, i, group, before, bi):
                for s in range(2):
                    if before is not None:
                        sp.wait_ge(lo_done, bi + (before.slab_ends(s) + 1 + PAN))
                    cols = P if S.kind == "down" else 2 * P
                    k = 11 if S.kind == "down" else 8
                    dst = raw[s][:, 0:k * cols].rearrange("p (k m) -> p k m", k=k)
                    sp.dma_start(dst, slab(S, i, group, s)).then_inc(raw_loaded[s], 16)

            def stage_loads(S, i, first):
                for group in range(S.groups):
                    if first and group == 0:
                        B = RUN[S.index - 1] if S.index else None
                        group_loads(S, i, group, B, S.panel0 - PAN)
                    else:
                        group_loads(S, i, group, S, panel(S, i, group * PAN - PAN))

            for S in RUN:
                stage_loads(S, 0, True)
                if S.name == "xbc":
                    sp.wait_ge(panel_used, S.panel0 + PAN)
                    sp.dma_start(inv_count[:], inv_in.rearrange("p (w t) -> p w t", w=4)).then_inc(mixer_loaded, 16)
                    sp.dma_start(dt_raw[:], in_w[0][:, 2560:2592].rearrange("(k p) m -> p k m", p=P)
                                 ).then_inc(mixer_loaded, 16)
                    sp.dma_start(pool_wt[:], pool_w[0].rearrange("g (k p) m -> p g k m", p=P)
                                 ).then_inc(mixer_loaded, 16)
                    sp.wait_ge(ada_summed, 16)
                    sp.dma_start(tri[:], const_in[:, P + GRID_W:].rearrange("p (a b) -> p a b", a=4)
                                 ).then_inc(tri_loaded, 16)
                if S.iters <= 2:
                    for i in range(1, S.iters):
                        stage_loads(S, i, False)
                else:
                    with sp.Fori(1, S.iters) as i:
                        stage_loads(S, i, False)
            sp.wait_ge(f_taken_dve, 2)
            sp.wait_ge(f_taken_act, 2)
            sp.dma_start(out.rearrange("b (c p) d -> p (b c) d", p=P), y_tok[:]).then_inc(stored, 16)
            sp.wait_ge(stored, 16)

        @block.gpsimd
        def _(pool):
            def ada_quarters(layer, b, n):
                for q in range(4):
                    pool.wait_ge(ada_step, n * 4 + (4 * q + 4))
                    src = ada_w[layer, q * 2 * P:(q + 1) * 2 * P, ds(b * ADA_COLS, ADA_COLS)]
                    pool.dma_start(ada_raw[q % 2][:], src.rearrange("(k p) m -> p k m", p=P)
                                   ).then_inc(ada_loaded[q % 2], 16)

            pool.wait_ge(first_loaded[ADA_FIRST - 1], 16)
            with pool.Fori(ADA_FIRST, 16) as b:
                ada_quarters(0, b, b * 4)
            plink = [0]

            def pchain(ins):
                plink[0] += 1
                ins.then_inc(pool_link, 1)
                pool.wait_ge(pool_link, plink[0])

            pool.wait_ge(conv_step, NCONV * TAPS + 2 * TAPS)
            pool.wait_ge(mixer_loaded, 48)
            for u in pool_u:
                ins = nc.gpsimd.memset(u[:], 0.0)
            pchain(ins)
            pool.sem_inc(mu_ready, 2)
            for c in range(KT):
                u, g = pool_u[c % 2], c // 2
                pool.wait_ge(pool_in_taken, c + 1)
                src, width, n, L = u, 1, 0, pw_len
                while width < WINDOWS[g]:
                    dst = pool_s[n % 2]
                    L -= width
                    pchain(nc.gpsimd.tensor_tensor(dst[:, :, 0:L], src[:, :, 0:L], src[:, :, width:width + L], ALU.add))
                    src, width, n = dst, 2 * width, n + 1
                a = PAD - WINDOWS[g] // 2
                t3 = pool_s[n % 2]
                pchain(nc.gpsimd.tensor_tensor(t3[:, :, 0:LAT], src[:, :, a:a + LAT],
                                               inv_count[:, g, :][:, None, :].to_broadcast([P, 2, LAT]), ALU.mult))
                nc.gpsimd.tensor_tensor(mu[c // 4][:, c % 4, :].rearrange("p (s t) -> p s t", s=2), t3[:, :, 0:LAT],
                                        u[:, :, PAD:PAD + LAT], ALU.subtract).then_inc(mu_ready, 1)
                pool.wait_ge(mu_ready, c + 3)
            pool.wait_ge(dt_vec, 1)
            pool.wait_ge(tri_loaded, 16)
            pool.wait_ge(panel_used, BY["mix_out"].panel0 + PAN)
            for u, (g, c, quad, d) in enumerate(UNITS):
                if u > 1:
                    pool.wait_ge(seg_mm, u - 1)
                h0 = d * HEADS + 8 * g + 4 * quad
                nc.gpsimd.tensor_tensor(seg_rhs[u % 2][:], dta[:, c, h0:h0 + 4][:, :, None].to_broadcast([P, 4, P]),
                                        tri[:, d, :][:, None, :].to_broadcast([P, 4, P]), ALU.mult
                                        ).then_inc(seg_ready, 1)
                n = u // 4 - 1 if u % 4 == 2 else CHUNKS * 2 - 1 if u == len(UNITS) - 1 else -1
                if n >= 0:
                    pool.wait_ge(z_done, 1)
                    pool.wait_ge(yt_done, n + 1)
                    y_t, z_t = (a[:, 4 * (n // CHUNKS):4 * (n // CHUNKS) + 4, (n % CHUNKS) * P:(n % CHUNKS + 1) * P]
                                for a in (xbc, zs))
                    nc.gpsimd.tensor_tensor(y_t, y_t, z_t, ALU.mult).then_inc(y_gated, 1)
            if len(RUN) > BY["ffn1_up"].index:
                pool.wait_ge(out_taken, BY["ffn1_up"].out0 + PAN)
                with pool.Fori(16, 18) as b:
                    ada_quarters(0, b, b * 4)
                with pool.Fori(0, 9 if len(RUN) <= BY["ffn2_up"].index else 18) as b:
                    ada_quarters(1, b, b * 4 + 18 * 4)
            if len(RUN) > BY["na_out"].index:
                pool.wait_ge(panel_used, BY["k"].panel0 + PAN)
                for t in range(2):
                    if t:
                        pool.wait_ge(masked, 1)
                    for r in range(2):
                        row = 2 * t + r
                        for key_row in range(ROWS):
                            src = bass.AP(tensor=rpb.tensor,
                                          offset=(key_row - row + 7) * RPB_C + WIN_C - GRID_W,
                                          ap=[[1, GRID_W], [RPB_R * RPB_C, HEADS], [1, GRID_W]])
                            pool.dma_start(bias_rev[r * GRID_W:(r + 1) * GRID_W, :, key_row, :], src
                                           ).then_inc(bias_loaded, 16)
                pool.wait_ge(out_taken, BY["na_out"].out0 + PAN)
                pool.wait_ge(panel_used, BY["na_out"].panel0 + PAN)
                pool.wait_ge(vt_done, 8)

                def stage_qk(t, b):
                    if not (isinstance(t, int) and t < 2):
                        pool.wait_ge(qk_mm, t * 4 - 4 + 1)
                    nc.gpsimd.tensor_copy(q_s[b][:], qt_all[:, ds(t, 1), :].rearrange("p a b -> p (a b)")
                                          ).then_inc(q_staged, 1)
                    nc.gpsimd.tensor_copy(k_s[b][:], kt_all[:, ds(t, 1), :].rearrange("p a b -> p (a b)")
                                          ).then_inc(q_staged, 1)

                def staging(t, b, more):
                    if more:
                        stage_qk(t + 1, 1 - b)
                    pool.wait_ge(pv_mm, t * 2 + 2)
                    nc.gpsimd.tensor_copy(v_s[:], v_tok[:, :, ds(t * P, P)]).then_inc(v_staged, 1)

                stage_qk(0, 0)
                head_pairs(pool, staging)

        @block.tensor
        def _(pe):
            pe.sem_inc(panel_used, PAN)
            pe.sem_inc(qk_mm, 1)
            pe.sem_inc(pv_mm, 2)
            pe.sem_inc(pt_mm, 4)
            pe.sem_inc(ada_summed, ADA_FIRST)

            def run_panel(S, i, j, first):
                slot, _, nk, _, o, part, k0 = S.panels[j]
                gp = panel(S, i, j)
                N = S.tokens
                acts = (g_hi, g_lo) if S.kind == "down" else (h_hi, h_lo)
                if S.opens(j) and part == 0:
                    pe.wait_ge(out_taken, output(S, i, o) - S.outs + (1 + PAN))
                pe.wait_ge(lo_done, gp + (1 + PAN))
                dst = bank(S, j)[:, 0:N]
                ends = S.closes(j) is not None or S.kind == "up"
                for k in range(nk):
                    gk = k0 + k
                    if S.kind == "mix":
                        acts = (y_hi, y_lo) if gk < KT else (pooled_hi, pooled_lo)
                    elif S.name == "na_out":
                        acts = (o_hi, o_lo)
                    a_hi, a_lo = acts[0][:, gk % KT if S.kind == "mix" else gk, 0:N], \
                        acts[1][:, gk % KT if S.kind == "mix" else gk, 0:N]
                    if first and o == 0 and part == 0 or (first and S.kind == "mix"):
                        if S.kind == "down":
                            pe.wait_ge(g_ready, RUN[S.index - 1].up0 + gk + 2)
                        elif S.kind == "mix" and gk < KT:
                            pe.wait_ge(y_ready, gk + 1)
                    w_hi, w_lo = pan_hi[j % PAN][:, k, :], pan_lo[j % PAN][:, k, :]
                    start = S.opens(j) and k == 0
                    stop = ends and k == nk - 1
                    pe.matmul(dst, w_hi, a_hi, start=start, stop=False)
                    pe.matmul(dst, w_hi, a_lo, start=False, stop=False)
                    mm = pe.matmul(dst, w_lo, a_hi, start=False, stop=stop)
                mm.then_inc(panel_used, 1)

            def run_after_norm(S):
                V = S.tokens // LAT
                for v in range(V):
                    sl = slice(v * LAT, (v + 1) * LAT)
                    for j in range(PAN):
                        if v == 0:
                            if S.opens(j) and S.panels[j][5] == 0:
                                pe.wait_ge(out_taken, output(S, 0, S.panels[j][4]) - S.outs + (1 + PAN))
                            pe.wait_ge(lo_done, panel(S, 0, j) + (1 + PAN))
                        for k in range(KT):
                            pe.wait_ge(h_hi_done, KT * (halves(S.norm) + v) + k + 1)
                            for n, w in enumerate((pan_hi, pan_lo)):
                                pe.matmul(bank(S, j)[:, sl], w[j % PAN][:, k, :], h_hi[:, k, sl],
                                          start=k == v == n == 0, stop=False, skip_group_check=True)
                for j in range(PAN):
                    for k in range(KT):
                        pe.wait_ge(h_ready, KT * (halves(S.norm) + V - 1) + k + 1)
                        mm = pe.matmul(bank(S, j)[:, 0:S.tokens], pan_hi[j % PAN][:, k, :], h_lo[:, k, 0:S.tokens],
                                       start=False, stop=k == KT - 1, skip_group_check=True)
                    mm.then_inc(panel_used, 1)

            def ada_sum(b):
                pe.wait_ge(ada_step, b * 16 + (16 + 8))
                pe.wait_ge(mods_done, b + 1)
                for ct in range(4):
                    for v in range(2):
                        mm = pe.matmul(ada_bank[:, 2 * ct + v:2 * ct + v + 1], ada_acc[:, v, ct * P:(ct + 1) * P],
                                       ones[:, 0:1], start=True, stop=True)
                mm.then_inc(ada_summed, 1)

            def stat(n, N):
                if n == BY["ffn3_up"].norm:
                    pe.wait_ge(out_taken, BY["ffn3_up"].out0 + PAN)
                pe.wait_ge(ssq_added, KT * (n + 1))
                pe.matmul(stat_bank[:, 0:N], ones[:], ssq[:, 0:N], start=True, stop=False)
                pe.wait_ge(square_done, KT * (n + 1))
                pe.matmul(stat_bank[:, 0:N], ones[:], tmp[0][:, 0:N], start=False, stop=True).then_inc(stat_done, 1)

            def dt_products():
                pe.wait_ge(dt_split, 1)
                for c in range(CHUNKS):
                    dst = ps[7][:, c * 32:c * 32 + 32]
                    for k in range(KT):
                        a_hi, a_lo = h_hi[:, k, c * P:(c + 1) * P], h_lo[:, k, c * P:(c + 1) * P]
                        pe.matmul(dst, a_hi, dt_hi[:, k, :], start=k == 0, stop=False)
                        pe.matmul(dst, a_hi, dt_lo[:, k, :], start=False, stop=False)
                        mm = pe.matmul(dst, a_lo, dt_hi[:, k, :], start=False, stop=k == KT - 1)
                mm.then_inc(dt_mm, 1)

            def pool_products(g0, banks):
                if g0:
                    pe.wait_ge(pool_hi, 4)
                    pe.wait_ge(pool_lo, 4)
                for g in (g0, g0 + 1):
                    pe.wait_ge(mu_ready, 2 * g + 4)
                    for t in range(2):
                        for k in range(2):
                            mm = pe.matmul(ps[banks + 2 * (g - g0) + t][:], pool_wt[:, g, k, t * P:(t + 1) * P],
                                           mu[g // 2][:, 2 * (g % 2) + k, :], start=k == 0, stop=k == 1)
                        mm.then_inc(pool_mm, 1)

            def turn(dst, src):
                return pe.transpose(dst, src, ident[:])

            def ssd():
                pe.wait_ge(dt_vec, 1)
                pe.wait_ge(tri_loaded, 16)
                pe.wait_ge(out_taken, BY["mix_out"].out0 + PAN)
                pe.wait_ge(pool_lo, 8)
                for which in range(3):
                    for c in range(CHUNKS):
                        for d in range(2):
                            lhs = (tri[:, d, :], tri[:, 2 + d, :], ones[:])[which]
                            at0 = which * P + c * 32 + d * HEADS
                            mm = pe.matmul(ps[4][:, at0:at0 + HEADS], lhs, dta[:, c, d * HEADS:(d + 1) * HEADS],
                                           start=True, stop=True)
                mm.then_inc(sums_mm, 1)
                u = yt = 0
                for g in range(2):
                    for c in range(CHUNKS):
                        pe.wait_ge(conv_done, NCONV + 2)
                        if g or c > 1:
                            pe.wait_ge(xd_done, 2 * (CHUNKS * g + c - 1))
                        for t in range(4):
                            mm = turn(ps[5 + c % 2][:, t * P:(t + 1) * P], xbc[:, 4 * g + t, c * P:(c + 1) * P])
                        mm.then_inc(xt_mm, 1)
                    if g == 0:
                        pe.wait_ge(exps_done, 1)
                    else:
                        pe.wait_ge(yt_done, CHUNKS)
                    for c in range(CHUNKS):
                        mm = turn(ps[4][:, c * P:(c + 1) * P], xbc[:, 8 + g, c * P:(c + 1) * P])
                    mm.then_inc(bt_mm, 1)
                    for c in range(CHUNKS):
                        mm = pe.matmul(ps[7][:, c * P:(c + 1) * P], xbc[:, 8 + g, c * P:(c + 1) * P],
                                       xbc[:, 10 + g, c * P:(c + 1) * P], start=True, stop=True)
                    mm.then_inc(cb_mm, 1)
                    pe.wait_ge(bt_done, g + 1)
                    pe.wait_ge(xd_done, 8 * (g + 1))
                    for n in range(6):
                        pos, d = n // 2, n % 2
                        c = ORDER[d][pos]
                        pe.wait_ge(xdd_done, 6 * g + n + 1)
                        if n > 1:
                            pe.wait_ge(state_done, 6 * g + n - 1)
                        pe.matmul(ps[5 + n % 2][:], b_tok[:, c, :], xdd[n % 2][:], start=True, stop=True
                                  ).then_inc(state_mm, 1)
                    pe.wait_ge(cb_done, 2 * (g + 1))
                    pe.wait_ge(state_done, 6 * (g + 1))
                    segments(16 * g)
                    for u in range(16 * g, 16 * g + 16):
                        c, n = u % 16 // 4, u % 4
                        if u % 16 < 15:
                            segments(u + 1)
                        diagonal(u, n, c)
                        if n == 0:
                            if c:
                                turn_y(CHUNKS * g + c - 1)
                            if u:
                                pe.wait_ge(y_sum, CHUNKS * g + c)
                            for d in range(2):
                                pos = ORDER[d].index(c)
                                if pos:
                                    mm = pe.matmul(ps[6 + d][:], xbc[:, 10 + g, c * P:(c + 1) * P],
                                                   states[d][:, pos - 1, :], start=True, stop=True)
                            mm.then_inc(off_mm, 1)
                    turn_y(CHUNKS * g + 3)

            def segments(u):
                pe.wait_ge(seg_ready, u + 1)
                if u > 1:
                    pe.wait_ge(decay_done, u - 1)
                pe.matmul(ps[u % 2][:], tri[:, 2 + UNITS[u][3], :], seg_rhs[u % 2][:].rearrange("p a b -> p (a b)"),
                          start=True, stop=True).then_inc(seg_mm, 1)

            def turn_y(n):
                pe.wait_ge(y_sum, n + 1)
                if n:
                    pe.wait_ge(yt_done, n)
                for t in range(4):
                    mm = turn(ps[4][:, t * P:(t + 1) * P], tmp[0][:, t * P:(t + 1) * P])
                mm.then_inc(yt_mm, 1)

            def diagonal(u, n, c):
                quad, d = n // 2, n % 2
                pe.wait_ge(weight_done, u + 1)
                for hh in range(4):
                    hx = 4 * quad + hh
                    mm = pe.matmul(ps[2 + c % 2][:, hx * HD:(hx + 1) * HD], weight[u % 2][:, hh, :],
                                   xd[d][:, c, hx * HD:(hx + 1) * HD], start=n == 0 and hh == 0,
                                   stop=n == 3 and hh == 3, skip_group_check=True)
                mm.then_inc(diag_mm, 1)

            def turn_v():
                pe.wait_ge(out_taken, BY["q"].out0 + PAN)
                for t in range(KT):
                    if t > 3:
                        pe.wait_ge(vt_done, t - 3)
                    for c in range(4):
                        mm = turn(ps[4 + t % 4][:, c * P:(c + 1) * P], vt_all[:, t, c * P:(c + 1) * P])
                    mm.then_inc(vt_mm, 1)

            def attention():
                pe.wait_ge(out_taken, BY["na_out"].out0 + PAN)
                pe.wait_ge(vt_done, 8)

                def scores(t, b, n):
                    a, qt = n // 2, n % 2
                    pe.wait_ge(q_staged, t * 2 + 2)
                    pe.wait_ge(s_ctx, t * 4 + (n + 1))
                    pe.wait_ge(s_done, t * 4 + (n + 1))
                    pe.matmul(ps[n][:], q_s[b][a * HD:(a + 1) * HD, qt * P:(qt + 1) * P],
                              k_s[b][a * HD:(a + 1) * HD, :], start=True, stop=True).then_inc(qk_mm, 1)

                def pair(t, b, more):
                    for a in range(2):
                        pe.wait_ge(pt_act, t * 2 + (a + 1))
                        pe.wait_ge(pt_dve, t * 2 + (a + 1))
                        for qt in range(2):
                            pe.wait_ge(p_norm, t * 4 + (2 * a + qt + 1))
                            for kt in range(4):
                                dst = ps[4 + kt // 2][:, (kt % 2) * LAT + qt * P:(kt % 2) * LAT + (qt + 1) * P]
                                mm = turn(dst, score[b][:, 2 * a + qt, kt * P:(kt + 1) * P])
                        mm.then_inc(pt_mm, 1)
                        if more:
                            scores(t + 1, 1 - b, 2 * a)
                            scores(t + 1, 1 - b, 2 * a + 1)
                        pe.wait_ge(pt_act, t * 2 + (a + 2))
                        pe.wait_ge(pt_dve, t * 2 + (a + 2))
                        if a == 0:
                            pe.wait_ge(v_staged, t + 1)
                            pe.wait_ge(o_done, t + 1)
                        for kt in range(4):
                            mm = pe.matmul(ps[6][a * HD:(a + 1) * HD, 0:LAT], v_s[:, kt, a * HD:(a + 1) * HD],
                                           prob_t[a][:, kt, :], start=kt == 0, stop=kt == 3)
                        mm.then_inc(pv_mm, 1)

                for n in range(4):
                    scores(0, 0, n)
                head_pairs(pe, pair)

            def ada_product(b, k):
                if k == 0:
                    pe.wait_ge(cond_done, 1)
                    pe.wait_ge(first_loaded[b], 16)
                mm = pe.matmul(ps[2 + b][0:2, :], cond[:, :, k], ada_first[:, b, k, :], start=k == 0, stop=k == KT - 1)
                if k == KT - 1:
                    mm.then_inc(rows_mm, 1)

            pe.wait_ge(x_loaded, 32)
            pe.wait_ge(const_loaded, 16)
            for t in range(KT):
                if t > 1:
                    pe.wait_ge(x_taken, t - 1)
                for c in range(4):
                    mm = turn(ps[t % 2][:, c * P:(c + 1) * P], x_in[:, c, t * P:(t + 1) * P])
                mm.then_inc(x_turned, 1)
                if t >= KT // 2:
                    for k in (2 * t - KT, 2 * t - KT + 1):
                        ada_product(0, k)
            pe.wait_ge(ones_done, 1)
            for b in range(1, ADA_FIRST):
                for k in range(KT):
                    ada_product(b, k)
                if b == 1:
                    stat(0, TOK)
            for b in range(ADA_FIRST):
                pe.wait_ge(rows_taken, b + 1)
                for t in range(4):
                    c = 4 * b + t
                    mm = pe.transpose(ada_bank[:, 2 * c:2 * c + 2], ada_rows[:, b, t * P:(t + 1) * P], ident[0:2, 0:2])
            mm.then_inc(rows_turned, 1)
            for S in RUN:
                if S.norm:
                    stat(S.norm, LAT if S.norm == 5 else TOK)
                if S.name == "pool_in":
                    dt_products()
                if S.name == "mix_out":
                    pool_products(2, 4)
                    ssd()
                    pe.wait_ge(yt_done, 2 * CHUNKS)
                if S.name == "na_out":
                    attention()
                    pe.wait_ge(o_done, 9)
                if S.norm is not None:
                    run_after_norm(S)
                for j in range(0 if S.norm is None else PAN, len(S.panels)):
                    if S.name == "pool_in" and j == 3:
                        pe.wait_ge(dt_taken, 1)
                    run_panel(S, 0, j, True)
                    if S.kind == "mix" and j == 0:
                        pe.wait_ge(gn_added, 8)
                        pe.matmul(stat_bank[:], ones[:], ssq[:], start=True, stop=True).then_inc(gn_stat, 1)
                if S.name == "ffn0_down":
                    ada_sum(14)
                    for j in range(len(S.panels)):
                        run_panel(S, 1, j, False)
                    ada_sum(15)
                cuts = [2 if S.name == "ffn0_down" else 1, S.iters]
                for a, b in zip(cuts, cuts[1:]):
                    if S.iters <= 2:
                        if S.name == "q":
                            turn_v()
                        if S.name == "z":
                            pe.wait_ge(out_taken, BY["z"].out0 + PAN)
                            pool_products(0, 4)
                        for j in range(len(S.panels)):
                            run_panel(S, 1, j, False)
                        continue
                    with pe.Fori(a, b) as i:
                        for j in range(len(S.panels)):
                            run_panel(S, i, j, False)
                            if S.ada and j == 2:
                                ada_sum(i + (S.ada - 1))
            stat(len([s for s in UPDATES if s in RUN]), LAT)
            for n in range(4):
                c, half = n // 2, n % 2
                pe.wait_ge(f_normed, KT)
                for t in range(4):
                    mm = turn(ps[n][:, t * P:(t + 1) * P], y_out[:, 4 * half + t, c * P:(c + 1) * P])
                mm.then_inc(f_turned, 1)

        @block.scalar
        def _(act):
            act.sem_inc(conv_done, 2)
            act.sem_inc(s_ctx, 4)
            act.sem_inc(pt_act, 1)
            link = [0]

            def square(q, og, t, N):
                act.wait_ge(out_taken, og) if og is not None else act.wait_ge(x_taken, q + 1)
                act.wait_ge(ssq_added, q + 1)
                nc.scalar.activation(tmp[0][:, 0:N], trunk[:, ds(t, 1), 0:N].rearrange("p a b -> p (a b)"),
                                     ACT.Square).then_inc(square_done, 1)

            def root(n, N):
                for v in range(N // LAT):
                    sl = slice(v * LAT, (v + 1) * LAT)
                    act.wait_ge(var_done, halves(n) + v + 1)
                    nc.scalar.activation(tmp[1][:, sl], tmp[0][:, sl], ACT.Sqrt).then_inc(root_done, 1)

            def norm(n, N, shift):
                if n:
                    root(n, N)
                for v in range(N // LAT):
                    sl = slice(v * LAT, (v + 1) * LAT)
                    for t in range(KT):
                        act.wait_ge(normed, KT * (halves(n) + v) + t + 1)
                        nc.scalar.activation(h_hi[:, t, sl], h_mid[:, t, sl], ACT.Identity,
                                             bias=mods[:, shift + t, v:v + 1]).then_inc(h_hi_done, 1)

            def tend(S, i, o):
                og = output(S, i, o)
                last = max(j for j in range(len(S.panels)) if S.panels[j][4] == o)
                N = S.tokens
                if S.kind == "up":
                    ug = i * 2 + (S.up0 + o)
                    act.wait_ge(panel_used, panel(S, i, last) + (1 + PAN))
                    act.wait_ge(out_taken, og + PAN)
                    nc.scalar.activation(tmp[0][:, 0:N], ps[S.bank0 + 2 * o][:, 0:N], ACT.Silu
                                         ).then_inc(silu_done, 1)
                    act.wait_ge(out_taken, og + (1 + PAN))
                    nc.scalar.activation(g_hi[:, ds(i * 2 + o, 1), 0:N].rearrange("p a b -> p (a b)"),
                                         tmp[1][:, 0:N], ACT.Copy).then_inc(g_hi_done, 1)
                elif S in UPDATES:
                    t = i * S.outs + o
                    square(t + KT * S.update, og + (1 + PAN), t, N)
                elif S.name == "xbc":
                    c = i * 4 + o
                    pad, acc = conv_pad[o % 2], tmp[o % 2]
                    act.wait_ge(panel_used, panel(S, i, last) + (1 + PAN))
                    act.wait_ge(conv_step, c * TAPS + TAPS)
                    nc.scalar.activation(pad[:, :, 2:2 + LAT], ps[S.bank0 + o][:].rearrange("p (s t) -> p s t", s=2),
                                         ACT.Copy).then_inc(out_taken, 1)
                    act.wait_ge(out_taken, og + (1 + PAN))
                    act.wait_ge(conv_done, c + 1)
                    nc.scalar.activation(acc[:].rearrange("p (s t) -> p s t", s=2), pad[:, :, 0:LAT], ACT.Identity,
                                         scale=vec[:, ds(c + VEC["conv_w"], 1)], bias=vec[:, ds(c + VEC["conv_b"], 1)]
                                         ).then_inc(conv_first, 1)
                    if not (isinstance(i, int) and c == 0):
                        conv_silu(c - 1, (o - 1) % 2)
                elif S.name == "pool_in":
                    c = i * 4 + o
                    act.wait_ge(panel_used, panel(S, i, last) + (1 + PAN))
                    act.wait_ge(mu_ready, c + 1)
                    nc.scalar.activation(pool_u[c % 2][:, :, PAD:PAD + LAT],
                                         ps[S.bank0 + o][:].rearrange("p (s t) -> p s t", s=2), ACT.Copy
                                         ).then_inc(out_taken, 1)
                    act.wait_ge(out_taken, og + (1 + PAN))
                    act.sem_inc(pool_in_taken, 1)

            def gn_squares(n):
                act.wait_ge(y_gated, n + 1)
                if n:
                    act.wait_ge(gn_added, n)
                g, c = n // CHUNKS, n % CHUNKS
                nc.scalar.activation(y_sq[:], xbc[:, 4 * g:4 * g + 4, c * P:(c + 1) * P], ACT.Square
                                     ).then_inc(gn_square, 1)

            def conv_silu(c, slot):
                act.wait_ge(conv_step, c * TAPS + 3 * TAPS)
                nc.scalar.activation(xbc[:, ds(c, 1), :].rearrange("p a b -> p (a b)"), tmp[slot][:], ACT.Silu
                                     ).then_inc(conv_done, 1)

            def pooled(n):
                act.wait_ge(pool_mm, n + 1)
                nc.scalar.activation(pooled_hi[:, n, :], ps[4 + n % 4][:], ACT.Copy,
                                     scale=vec[:, VEC["pool_scale"] + n:VEC["pool_scale"] + n + 1]
                                     ).then_inc(pool_hi, 1)

            def step(S, i, j, prior, first):
                if silu_first(S, j, first):
                    tend(*prior)
                    prior = None
                if S is not None:
                    slot, k0, nk, c0, _, _, _ = S.panels[j]
                    down = S.kind == "down"
                    group = i * S.groups + (S.group0 + j // PAN)
                    act.wait_ge(raw_loaded[slot], group * 16 + 16)
                    act.wait_ge(panel_used, panel(S, i, j) + 1)
                    src = raw[slot][:, 0:(11 * P if down else 16 * P)].rearrange("p (k m) -> p k m", k=11 if down else 8)
                    nc.scalar.activation(pan_hi[j % PAN][:, 0:nk, :], src[:, k0:k0 + nk, c0:c0 + P], ACT.Copy
                                         ).then_inc(hi_done, 1)
                if first and j == LAG and normed_stage(S):
                    after(RUN[S.index - 1].name if S.index else "start", S)
                if prior is not None:
                    tend(*prior)
                if first and j == LAG - 1 and not normed_stage(S):
                    after(RUN[S.index - 1].name if S is not None and S.index else "end", S)
                if S is not None and S.name == "z" and not first and j == PAN - 1:
                    for n in range(4):
                        pooled(n)

            def after(name, S):
                if name == "xbc":
                    conv_silu(NCONV - 1, (NCONV - 1) % 2)
                    act.wait_ge(dt_abs, 1)
                    nc.scalar.activation(dt_b[:], dt_a[:], ACT.Exp, scale=-1.0).then_inc(dt_act, 1)
                    nc.scalar.activation(a_coef[:], vec[:, VEC["a_log"]:VEC["a_log"] + 32], ACT.Exp
                                         ).then_inc(dt_act, 1)
                if name == "z":
                    act.wait_ge(out_taken, BY["mix_out"].out0 + PAN)
                    nc.scalar.activation(zs[:], zs[:], ACT.Silu).then_inc(z_done, 1)
                    for n in range(4, 8):
                        pooled(n)
                    act.wait_ge(sums_mm, 1)
                    nc.scalar.activation(exps[:].rearrange("p a b c -> p (a b c)"), ps[4][:, 0:3 * P], ACT.Exp
                                         ).then_inc(exps_done, 1)
                    for u in range(len(UNITS)):
                        act.wait_ge(seg_mm, u + 1)
                        if u > 1:
                            act.wait_ge(weight_done, u - 1)
                        nc.scalar.activation(decay[u % 2][:].rearrange("p a b -> p (a b)"), ps[u % 2][:], ACT.Exp
                                             ).then_inc(decay_done, 1)
                        if u % 4 == 3 and u > 3:
                            gn_squares(u // 4 - 1)
                    gn_squares(CHUNKS * 2 - 1)
                    act.wait_ge(gn_var, 1)
                    nc.scalar.activation(tmp[1][:], tmp[0][:], ACT.Sqrt).then_inc(gn_root, 1)
                    for t in range(KT):
                        act.wait_ge(y_gated, KT + t + 1)
                        nc.scalar.activation(y_hi[:, t, :], xbc[:, t, :], ACT.Copy).then_inc(y_hi_done, 1)
                if name == "q":
                    def soften(t, b, a):
                        for n in (2 * a, 2 * a + 1):
                            act.wait_ge(qk_mm, t * 4 + (n + 2))
                            act.wait_ge(pt_mm, t * 2 + (a + 1))
                            nc.scalar.activation(score[b][:, n, LAT:TOK], ps[n][:, LAT:TOK], ACT.Copy,
                                                 scale=HD ** -0.5).then_inc(s_ctx, 1)
                        for n in (2 * a, 2 * a + 1):
                            act.wait_ge(max_done, t * 4 + (n + 1))
                            nc.scalar.activation(score[b][:, n, :], score[b][:, n, :], ACT.Exp, bias=smax[:, n, 1:2],
                                                 accum_out=smax[:, n, 2:3]).then_inc(p_done, 1)

                    def pair(t, b, more):
                        for a in range(2):
                            act.wait_ge(pt_mm, t * 2 + (a + 5))
                            nc.scalar.activation(prob_t[a][:, 0:2, :].rearrange("p a b -> p (a b)"), ps[4][:], ACT.Copy
                                                 ).then_inc(pt_act, 1)
                            if more:
                                soften(t + 1, 1 - b, a)
                        act.wait_ge(pv_mm, t * 2 + 4)
                        nc.scalar.activation(o_hi[:, ds(t, 1), :].rearrange("p a b -> p (a b)"), ps[6][:, 0:LAT],
                                             ACT.Copy).then_inc(o_hi_done, 1)

                    soften(0, 0, 0)
                    soften(0, 0, 1)
                    head_pairs(act, pair)
                if S is not None and S.norm is not None:
                    norm(S.norm, S.tokens, (S.norm // 3) * 72 + 24 * (S.norm % 3))
                if name == "ffn0_down":
                    act.wait_ge(mixer_loaded, 48)
                    nc.scalar.activation(dt_hi[:], dt_raw[:], ACT.Copy).then_inc(dt_hi_done, 1)
                if name == "end":
                    root(len([s for s in UPDATES if s in RUN]), LAT)
                    for n in range(2):
                        act.wait_ge(f_turned, 2 * n + 2)
                        nc.scalar.activation(y_tok[:, n, 512:1024], ps[2 * n + 1][:], ACT.Copy
                                             ).then_inc(f_taken_act, 1)

            act.wait_ge(vec_loaded, 16)
            nc.scalar.activation(cond[:].rearrange("p a b -> p (a b)"), vec[:, 0:16], ACT.Silu).then_inc(cond_done, 1)
            for t in range(KT):
                square(t, None, t, TOK)
            root(0, TOK)
            walk(act, step)

        @block.vector
        def _(dve):
            link = [0]

            def chain(ins):
                link[0] += 1
                ins.then_inc(dve_link, 1)
                dve.wait_ge(dve_link, link[0])

            def tt(o, a, b, op):
                return nc.vector.tensor_tensor(o, a, b, op)

            nc.vector.memset(ones[:], 1.0).then_inc(ones_done, 1)
            dve.wait_ge(ones_done, 1)
            chain(nc.vector.memset(ssq[:], 0.0))
            dve.sem_inc(lo_done, PAN)
            dve.sem_inc(out_taken, PAN)
            dve.sem_inc(ssq_added, 1)
            dve.sem_inc(ada_step, 8 + 16 * ADA_FIRST)
            dve.sem_inc(g_ready, 1)
            dve.sem_inc(mods_done, 1)
            dve.sem_inc(s_done, 4)
            dve.sem_inc(pt_dve, 1)
            dve.sem_inc(o_done, 1)

            def add_square(q, N):
                if isinstance(q, int) and q % KT == KT - 1:
                    dve.wait_ge(square_done, q + 1)
                    dve.sem_inc(ssq_added, 1)
                    return
                dve.wait_ge(square_done, q + 1)
                dve.wait_ge(ssq_added, q + 1)
                tt(ssq[:, 0:N], ssq[:, 0:N], tmp[0][:, 0:N], ALU.add).then_inc(ssq_added, 1)

            def ada_quarter(b, q):
                dve.wait_ge(ada_loaded[q % 2], (b - ADA_FIRST) * 32 + ((q // 2) * 16 + 16))
                for kk in range(2):
                    for v in range(2):
                        n = 4 * q + 2 * kk + v
                        k = 2 * q + kk
                        dve.wait_ge(ada_step, b * 16 + (n - 2 + 1 + 8))
                        if n < 2:
                            ins = nc.vector.tensor_scalar(ada_acc[:, v, :], ada_raw[q % 2][:, kk, :],
                                                          cond[:, v, k:k + 1], None, ALU.mult)
                        else:
                            ins = nc.vector.scalar_tensor_tensor(out=ada_acc[:, v, :], in0=ada_raw[q % 2][:, kk, :],
                                                                 scalar=cond[:, v, k:k + 1], in1=ada_acc[:, v, :],
                                                                 op0=ALU.mult, op1=ALU.add)
                        ins.then_inc(ada_step, 1)

            def ada_take(b):
                dve.wait_ge(ada_summed, b + 1)
                tt(mods[:, ds(b * 4, 4), :], ada_bank[:, 0:8].rearrange("p (t v) -> p t v", v=2),
                   vec[:, ds(b * 4 + VEC["ada_b"], 4)][:, :, None].to_broadcast([P, 4, 2]), ALU.add
                   ).then_inc(mods_done, 1)

            def set_gate(l, chunk, factor):
                c0 = l * 72 + chunk * 8
                dve.wait_ge(mods_done, (c0 + 8) // 4 + 1)
                chain(nc.vector.tensor_scalar(gate[:], mods[:, c0:c0 + 8, :], factor, None, ALU.mult))

            def variance(n, N):
                dve.wait_ge(stat_done, n + 1)
                for v in range(N // LAT):
                    sl = slice(v * LAT, (v + 1) * LAT)
                    nc.vector.tensor_scalar(tmp[0][:, sl], stat_bank[:, sl], 1.0 / D, EPS, ALU.mult, ALU.add
                                            ).then_inc(var_done, 1)

            def inverse_root(n, v):
                sl = slice(v * LAT, (v + 1) * LAT)
                dve.wait_ge(root_done, halves(n) + v + 1)
                chain(nc.vector.reciprocal(ssq[:, sl], tmp[1][:, sl]))

            def norm(n, N):
                l, s = n // 3, n % 3
                sc = l * 72 + (3 * s + 1) * 8
                sh = l * 72 + 3 * s * 8
                V = N // LAT
                dve.wait_ge(mods_done, (sc + 8) // 4 + 1)
                g0 = VEC["norm_g"] + n * 8
                chain(nc.vector.scalar_tensor_tensor(out=norm_scale[:], in0=mods[:, sc:sc + 8, :], scalar=1.0,
                                                     in1=vec[:, g0:g0 + 8][:, :, None].to_broadcast([P, 8, 2]),
                                                     op0=ALU.add, op1=ALU.mult))
                if n:
                    variance(n, N)
                for v in range(V):
                    sl = slice(v * LAT, (v + 1) * LAT)
                    if n:
                        inverse_root(n, v)
                    for t in range(KT):
                        nc.vector.scalar_tensor_tensor(out=h_mid[:, t, sl], in0=trunk[:, t, sl],
                                                       scalar=norm_scale[:, t, v:v + 1], in1=ssq[:, sl],
                                                       op0=ALU.mult, op1=ALU.mult).then_inc(normed, 1)
                for v in range(V):
                    sl = slice(v * LAT, (v + 1) * LAT)
                    for t in range(KT):
                        dve.wait_ge(h_hi_done, KT * (halves(n) + v) + t + 1)
                        nc.vector.scalar_tensor_tensor(out=h_lo[:, t, sl], in0=h_mid[:, t, sl],
                                                       scalar=mods[:, sh + t, v:v + 1],
                                                       in1=h_hi[:, t, sl].bitcast(F32),
                                                       op0=ALU.add, op1=ALU.subtract).then_inc(h_ready, 1)
                chain(nc.vector.memset(ssq[:], 0.0))

            def update(S, i, o):
                og, t = output(S, i, o), i * S.outs + o
                b = ps[S.bank0 + o]
                for v in range(S.tokens // LAT):
                    sl = slice(v * LAT, (v + 1) * LAT)
                    x_t = trunk[:, ds(t, 1), sl].rearrange("p a b -> p (a b)")
                    ins = nc.vector.scalar_tensor_tensor(out=x_t, in0=b[:, sl],
                                                         scalar=gate[:, ds(t, 1), v:v + 1].rearrange("p a b -> p (a b)"),
                                                         in1=x_t, op0=ALU.mult, op1=ALU.add)
                ins.then_inc(out_taken, 1)
                add_square(t + KT * S.update, S.tokens)

            def conv(S, i, o):
                c = i * 4 + o
                pad = conv_pad[o % 2]
                acc3 = tmp[o % 2][:].rearrange("p (s t) -> p s t", s=2)
                for j in range(1, CONV):
                    dve.wait_ge(*((conv_first, c + 1) if j == 1 else (conv_step, c * TAPS + (j - 1 + 2 * TAPS))))
                    nc.vector.scalar_tensor_tensor(out=acc3, in0=pad[:, :, j:j + LAT],
                                                   scalar=vec[:, ds(c + (VEC["conv_w"] + j * NCONV), 1)], in1=acc3,
                                                   op0=ALU.mult, op1=ALU.add).then_inc(conv_step, 1)

            def pooled(n):
                dve.wait_ge(pool_hi, n + 1)
                if n >= 4:
                    dve.wait_ge(pool_mm, 8)
                nc.vector.scalar_tensor_tensor(out=pooled_lo[:, n, :], in0=ps[4 + n % 4][:],
                                               scalar=vec[:, VEC["pool_scale"] + n:VEC["pool_scale"] + n + 1],
                                               in1=pooled_hi[:, n, :].bitcast(F32), op0=ALU.mult, op1=ALU.subtract
                                               ).then_inc(pool_lo, 1)

            def dt_steps():
                dve.wait_ge(dt_mm, 1)
                def over_chunks(a):
                    return a[:, None, :].to_broadcast([P, CHUNKS, 32])
                tt(dt_x[:], ps[7][:, 0:P].rearrange("p (c h) -> p c h", c=CHUNKS),
                   over_chunks(vec[:, VEC["dt_bias"]:VEC["dt_bias"] + 32]), ALU.add).then_inc(dt_taken, 1)
                dve.wait_ge(dt_taken, 1)

                def stt(o, a, s, b, op0, op1):
                    return nc.vector.scalar_tensor_tensor(out=o[:], in0=a[:], scalar=s, in1=b, op0=op0, op1=op1)

                stt(dt_a, dt_x, -1.0, dt_x[:], ALU.mult, ALU.max).then_inc(dt_abs, 1)
                dve.wait_ge(dt_act, 2)
                chain(nc.vector.tensor_scalar(dt_a[:], dt_b[:], 2.0, None, ALU.add))
                chain(nc.vector.reciprocal(dt_c[:], dt_a[:]))
                chain(tt(dt_a[:], dt_b[:], dt_c[:], ALU.mult))
                chain(tt(dt_b[:], dt_a[:], dt_a[:], ALU.mult))
                chain(nc.vector.tensor_scalar(dt_c[:], dt_b[:], 1.0 / 17, None, ALU.mult))
                for k in range(7, 0, -1):
                    chain(stt(dt_c, dt_c, 1.0 / (2 * k + 1), dt_b[:], ALU.add, ALU.mult))
                chain(stt(dt_c, dt_c, 1.0, dt_a[:], ALU.add, ALU.mult))
                chain(nc.vector.tensor_scalar(dt_c[:], dt_c[:], 2.0, None, ALU.mult))
                chain(stt(dt, dt_x, 0.0, dt_c[:], ALU.max, ALU.add))
                stt(dta, dt, -1.0, over_chunks(a_coef[:]), ALU.mult, ALU.mult).then_inc(dt_vec, 1)
                dve.wait_ge(dt_vec, 1)

            def ssd():
                def by_head(a, c, d, g):
                    return a[:, c, d * HEADS + 8 * g:d * HEADS + 8 * g + 8][:, :, None].to_broadcast([P, 8, HD])

                def heads(a):
                    return a.rearrange("p (h e) -> p h e", h=8)

                def over_heads(a):
                    return a[:, None, :].to_broadcast([P, 4, P])

                dve.wait_ge(tri_loaded, 16)

                def offs(g, c):
                    dve.wait_ge(off_mm, CHUNKS * g + c + 1)
                    if g or c:
                        dve.wait_ge(yt_mm, CHUNKS * g + c)
                    on = [d for d in range(2) if ORDER[d].index(c)]
                    for d in on:
                        chain(tt(heads(tmp[on.index(d)][:]), heads(ps[6 + d][:]), by_head(exps[:, 0], c, d, g),
                                 ALU.mult))
                    if len(on) > 1:
                        chain(tt(tmp[0][:], tmp[0][:], tmp[1][:], ALU.add))

                def finish(n):
                    dve.wait_ge(diag_mm, 4 * n + 4)
                    tt(tmp[0][:], tmp[0][:], ps[2 + n % 2][:], ALU.add).then_inc(y_sum, 1)

                def skip(n):
                    g, c = n // CHUNKS, n % CHUNKS
                    dve.wait_ge(yt_mm, n + 1)
                    for t in range(4):
                        d0 = VEC["d_skip"] + 4 * g + t
                        x_t = xbc[:, 4 * g + t, c * P:(c + 1) * P]
                        ins = nc.vector.scalar_tensor_tensor(out=x_t, in0=x_t, scalar=vec[:, d0:d0 + 1],
                                                             in1=ps[4][:, t * P:(t + 1) * P],
                                                             op0=ALU.mult, op1=ALU.add)
                    ins.then_inc(yt_done, 1)

                def add_squares(n):
                    g, c = n // CHUNKS, n % CHUNKS
                    dve.wait_ge(gn_square, n + 1)
                    part = ssq[:, c * P:(c + 1) * P]
                    if g == 0:
                        nc.vector.tensor_reduce(part, y_sq[:].rearrange("p a b -> p b a"), AX_X, ALU.add
                                                ).then_inc(gn_added, 1)
                    else:
                        more = dt_x[:].rearrange("p a b -> p (a b)")
                        chain(nc.vector.tensor_reduce(more, y_sq[:].rearrange("p a b -> p b a"), AX_X, ALU.add))
                        tt(part, part, more, ALU.add).then_inc(gn_added, 1)

                for g in range(2):
                    for c in range(CHUNKS):
                        dve.wait_ge(xt_mm, CHUNKS * g + c + 1)
                        for d in range(2):
                            tt(heads(xd[d][:, c, :]), heads(ps[5 + c % 2][:]), by_head(dt, c, d, g), ALU.mult
                               ).then_inc(xd_done, 1)
                    dve.wait_ge(bt_mm, g + 1)
                    nc.vector.tensor_copy(b_tok[:].rearrange("p a b -> p (a b)"), ps[4][:]).then_inc(bt_done, 1)
                    dve.wait_ge(cb_mm, g + 1)
                    for d in range(2):
                        tt(cb[d][:], ps[7][:].rearrange("p (a b) -> p a b", a=CHUNKS), over_heads(tri[:, d, :]),
                           ALU.mult).then_inc(cb_done, 1)
                    dve.wait_ge(exps_done, 1)
                    dve.wait_ge(xd_done, 8 * (g + 1))

                    def decayed(n):
                        pos, d = n // 2, n % 2
                        c = ORDER[d][pos]
                        if n > 1:
                            dve.wait_ge(state_mm, 6 * g + n - 1)
                        tt(heads(xdd[n % 2][:]), heads(xd[d][:, c, :]), by_head(exps[:, 1], c, d, g), ALU.mult
                           ).then_inc(xdd_done, 1)

                    decayed(0)
                    for n in range(6):
                        pos, d = n // 2, n % 2
                        c = ORDER[d][pos]
                        if n < 5:
                            decayed(n + 1)
                        dve.wait_ge(state_mm, 6 * g + n + 1)
                        if pos == 0:
                            nc.vector.tensor_copy(states[d][:, 0, :], ps[5 + n % 2][:]).then_inc(state_done, 1)
                        else:
                            dve.wait_ge(state_done, 6 * g + n)
                            chain(tt(heads(tmp[1][:]), heads(states[d][:, pos - 1, :]), by_head(exps[:, 2], c, d, g),
                                     ALU.mult))
                            tt(states[d][:, pos, :], tmp[1][:], ps[5 + n % 2][:], ALU.add).then_inc(state_done, 1)
                    for u in range(16 * g, 16 * g + 16):
                        c, n, done = u % 16 // 4, u % 4, u // 4
                        dve.wait_ge(decay_done, u + 1)
                        if u > 1:
                            dve.wait_ge(diag_mm, u - 1)
                        tt(weight[u % 2][:], decay[u % 2][:], over_heads(cb[n % 2][:, c, :]), ALU.mult
                           ).then_inc(weight_done, 1)
                        if n == 0 and c:
                            finish(done - 1)
                        if n == 0 and done > 1:
                            add_squares(done - 2)
                        if n == 1 and c:
                            skip(done - 1)
                        if n == 2:
                            offs(g, c)
                    finish(CHUNKS * g + 3)
                    skip(CHUNKS * g + 3)
                add_squares(CHUNKS * 2 - 2)
                add_squares(CHUNKS * 2 - 1)
                dve.wait_ge(gn_stat, 1)
                nc.vector.tensor_scalar(tmp[0][:], stat_bank[:], 1.0 / D, EPS, ALU.mult, ALU.add).then_inc(gn_var, 1)
                dve.wait_ge(gn_root, 1)
                chain(nc.vector.reciprocal(ssq[:], tmp[1][:]))
                def scaled(t):
                    g0 = VEC["gn_g"] + t
                    nc.vector.scalar_tensor_tensor(out=xbc[:, t, :], in0=xbc[:, t, :], scalar=vec[:, g0:g0 + 1],
                                                   in1=ssq[:], op0=ALU.mult, op1=ALU.mult).then_inc(y_gated, 1)

                scaled(0)
                for t in range(KT):
                    if t + 1 < KT:
                        scaled(t + 1)
                    dve.wait_ge(y_hi_done, t + 1)
                    tt(y_lo[:, t, :], xbc[:, t, :], y_hi[:, t, :].bitcast(F32), ALU.subtract).then_inc(y_ready, 1)
                chain(nc.vector.memset(ssq[:], 0.0))

            def attention():
                dve.wait_ge(masked, 2)

                def soften(t, b, a):
                    rows = (2 * a, 2 * a + 1)
                    for n in rows:
                        dve.wait_ge(s_ctx, t * 4 + (n + 5))
                        nc.vector.scalar_tensor_tensor(
                            out=score[b][:, n, 0:LAT].rearrange("p (r c) -> p r c", r=ROWS),
                            in0=ps[n][:, 0:LAT].rearrange("p (r c) -> p r c", r=ROWS), scalar=HD ** -0.5,
                            in1=bias[:, n % 2, ds(t * 2 + a, 1), :, :].rearrange("p h r c -> p (h r) c"),
                            op0=ALU.mult, op1=ALU.add).then_inc(s_done, 1)
                    for n in rows:
                        dve.wait_ge(s_done, t * 4 + (n + 5))
                        nc.vector.reduce_max(smax[:, n, 0:1], score[b][:, n, :], AX_X).then_inc(max_found, 1)
                        dve.wait_ge(max_found, t * 4 + (n + 1))
                        nc.vector.tensor_scalar(smax[:, n, 1:2], smax[:, n, 0:1], -1.0, None, ALU.mult
                                                ).then_inc(max_done, 1)
                    for n in rows:
                        dve.wait_ge(p_done, t * 4 + (n + 1))
                        nc.vector.reciprocal(smax[:, n, 3:4], smax[:, n, 2:3]).then_inc(sum_inverted, 1)
                        dve.wait_ge(sum_inverted, t * 4 + (n + 1))
                        nc.vector.tensor_scalar(score[b][:, n, :], score[b][:, n, :], smax[:, n, 3:4], None, ALU.mult
                                                ).then_inc(p_norm, 1)

                def pair(t, b, more):
                    for a in range(2):
                        dve.wait_ge(pt_mm, t * 2 + (a + 5))
                        nc.vector.tensor_copy(prob_t[a][:, 2:4, :].rearrange("p a b -> p (a b)"), ps[5][:]
                                              ).then_inc(pt_dve, 1)
                        if more:
                            soften(t + 1, 1 - b, a)
                    dve.wait_ge(pv_mm, t * 2 + 4)
                    dve.wait_ge(o_hi_done, t + 1)
                    tt(o_lo[:, ds(t, 1), :].rearrange("p a b -> p (a b)"), ps[6][:, 0:LAT],
                       o_hi[:, ds(t, 1), :].bitcast(F32).rearrange("p a b -> p (a b)"), ALU.subtract
                       ).then_inc(o_done, 1)

                soften(0, 0, 0)
                soften(0, 0, 1)
                head_pairs(dve, pair)

            def tend(S, i, o):
                og = output(S, i, o)
                last = max(j for j in range(len(S.panels)) if S.panels[j][4] == o)
                if S.kind == "up":
                    ug = i * 2 + (S.up0 + o)
                    N = S.tokens
                    dve.wait_ge(panel_used, panel(S, i, last) + (1 + PAN))
                    dve.wait_ge(silu_done, ug + 1)
                    dve.wait_ge(g_ready, ug + 1)
                    tt(tmp[1][:, 0:N], tmp[0][:, 0:N], ps[S.bank0 + 2 * o + 1][:, 0:N], ALU.mult
                       ).then_inc(out_taken, 1)

                    dve.wait_ge(g_hi_done, ug + 1)
                    g_t = ds(i * 2 + o, 1)
                    tt(g_lo[:, g_t, 0:N].rearrange("p a b -> p (a b)"), tmp[1][:, 0:N],
                       g_hi[:, g_t, 0:N].bitcast(F32).rearrange("p a b -> p (a b)"), ALU.subtract
                       ).then_inc(g_ready, 1)
                    return
                dve.wait_ge(panel_used, panel(S, i, last) + (1 + PAN))
                if S in UPDATES:
                    update(S, i, o)
                elif S.name == "xbc":
                    conv(S, i, o)
                elif S.name == "pool_in":
                    return
                else:
                    if S.name == "z" and i == 0 and o == 0:
                        dve.wait_ge(mu_ready, KT + 2)
                    dst = {"z": zs, "k": kt_all, "v": vt_all, "q": qt_all}[S.name]
                    N = S.tokens
                    nc.vector.tensor_copy(dst[:, 4 * i + o, 0:N], ps[S.bank0 + o][:, 0:N]).then_inc(out_taken, 1)

            def step(S, i, j, prior, first):
                if silu_first(S, j, first):
                    tend(*prior)
                    prior = None
                if S is not None:
                    slot, k0, nk, c0, _, _, _ = S.panels[j]
                    down = S.kind == "down"
                    dve.wait_ge(hi_done, panel(S, i, j) + 1)
                    src = raw[slot][:, 0:(11 * P if down else 16 * P)].rearrange("p (k m) -> p k m", k=11 if down else 8)
                    tt(pan_lo[j % PAN][:, 0:nk, :], src[:, k0:k0 + nk, c0:c0 + P],
                       pan_hi[j % PAN][:, 0:nk, :].bitcast(F32), ALU.subtract).then_inc(lo_done, 1)
                B = RUN[S.index - 1] if S is not None and S.index and first else None
                if S is not None and S.ada and not first:
                    if isinstance(i, int) and i == 1:
                        if j in (1, 2):
                            ada_quarter(S.ada, j)
                    else:
                        if j == 0:
                            ada_quarter(i + (S.ada - 2), 3)
                        if j == 1:
                            ada_take(i + (S.ada - 2))
                        if j >= 1:
                            ada_quarter(i + (S.ada - 1), j - 1)
                elif B and B.ada and j == 0:
                    ada_quarter(B.ada + B.iters - 2, 3)
                elif S is not None and S.name == "ffn0_down" and isinstance(i, int) and i < 2:
                    if i == 1 and j == 2:
                        ada_take(14)
                    if LAG <= j < LAG + 4:
                        ada_quarter(14 + i, j - LAG)
                if first and j == LAG and normed_stage(S):
                    after(RUN[S.index - 1].name if S.index else "start", S)
                    if S.ada:
                        ada_quarter(S.ada, 0)
                if prior is not None:
                    tend(*prior)
                if S is not None and S.name == "z" and not first and j == PAN - 1:
                    for n in range(4):
                        pooled(n)
                if S is not None and S.name == "q" and not first and j == LAG - 1:
                    for t in range(KT):
                        dve.wait_ge(vt_mm, t + 1)
                        nc.vector.tensor_copy(v_tok[:, :, t * P:(t + 1) * P],
                                              ps[4 + t % 4][:].rearrange("p (c e) -> p c e", c=4)).then_inc(vt_done, 1)
                if first and j == LAG - 1 and not normed_stage(S):
                    after(RUN[S.index - 1].name if S is not None and S.index else "end", S)

            def after(name, S):
                if name.endswith("_up"):
                    A = BY[name]
                    if A.ada:
                        ada_take(A.ada + A.iters - 2)
                    l, half = A.arg
                    set_gate(l, 2 if half == 0 else 8, 0.5)
                if name == "ffn0_down":
                    ada_take(15)
                if name == "xbc":
                    dt_steps()
                if name == "z":
                    for n in range(4, 8):
                        pooled(n)
                    ssd()
                    set_gate(0, 5, 1.0)
                if name in ("k", "v"):
                    half = int(name == "v")
                    dve.wait_ge(bias_loaded, 128 * (half + 1))
                    dve.wait_ge(mask_loaded, 16)
                    tt(bias[:, half, :, :, :].rearrange("p h r c -> p (h r) c"),
                       bias_rev[:, :, :, ::-1].rearrange("p h r c -> p (h r) c"),
                       na_mask[:, None, :].to_broadcast([P, HEADS * ROWS, GRID_W]), ALU.add).then_inc(masked, 1)
                if name == "q":
                    attention()
                    set_gate(1, 5, 1.0)
                if S is not None and S.norm is not None:
                    norm(S.norm, S.tokens)
                if name == "ffn0_down":
                    for pad in conv_pad:
                        chain(nc.vector.memset(pad[:], 0.0))
                    dve.sem_inc(conv_step, 2 * TAPS)
                    dve.wait_ge(dt_hi_done, 1)
                    tt(dt_lo[:], dt_raw[:], dt_hi[:].bitcast(F32), ALU.subtract).then_inc(dt_split, 1)
                if name == "end":
                    n = len([s for s in UPDATES if s in RUN])
                    variance(n, LAT)
                    inverse_root(n, 0)
                    for t in range(KT):
                        g0 = VEC["final_g"] + t
                        nc.vector.scalar_tensor_tensor(out=y_out[:, t, :], in0=trunk[:, t, 0:LAT],
                                                       scalar=vec[:, g0:g0 + 1], in1=ssq[:, 0:LAT],
                                                       op0=ALU.mult, op1=ALU.mult).then_inc(f_normed, 1)
                    for n in range(2):
                        dve.wait_ge(f_turned, 2 * n + 1)
                        nc.vector.tensor_copy(y_tok[:, n, 0:512], ps[2 * n][:]).then_inc(f_taken_dve, 1)

            for t in range(KT):
                dve.wait_ge(x_turned, t + 1)
                nc.vector.tensor_copy(trunk[:, t, :], ps[t % 2][:]).then_inc(x_taken, 1)
                add_square(t, TOK)
            variance(0, TOK)
            inverse_root(0, 0)
            inverse_root(0, 1)
            for b in range(ADA_FIRST):
                dve.wait_ge(rows_mm, b + 1)
                nc.vector.tensor_copy(ada_rows[:, b, :], ps[2 + b][0:2, :]).then_inc(rows_taken, 1)
            dve.wait_ge(rows_turned, 1)
            nt = ADA_FIRST * 4
            tt(mods[:, 0:nt, :], ada_bank[:, 0:2 * nt].rearrange("p (t v) -> p t v", v=2),
               vec[:, VEC["ada_b"]:VEC["ada_b"] + nt][:, :, None].to_broadcast([P, nt, 2]), ALU.add
               ).then_inc(mods_done, ADA_FIRST)
            walk(dve, step)


def kernel(x, c, ctx, c_ctx, ada_w, ada_b, norm_g, ffn_w1, ffn_w3, ffn_w2, ssd_in_w, ssd_conv_w, ssd_conv_b,
           ssd_dt_bias, ssd_a_log, ssd_d, ssd_norm_g, pool_w, pool_scale, mix_a_out_w, na_qkv_w, na_rpb, na_out_w,
           final_norm_g):
    import concourse.bacc as bacc
    from concourse.bass_utils import run_bass_kernel_spmd

    def columns(a):
        return np.asarray(a).reshape(-1, P).T

    rows = {"c": columns(c), "c_ctx": columns(c_ctx), "norm_g": columns(norm_g), "ada_b": columns(ada_b),
            "conv_b": columns(ssd_conv_b), "conv_w": columns(ssd_conv_w), "gn_g": columns(ssd_norm_g),
            "pool_scale": columns(pool_scale), "d_skip": columns(np.repeat(np.asarray(ssd_d), HD)),
            "final_g": columns(final_norm_g),
            "dt_bias": np.broadcast_to(np.asarray(ssd_dt_bias).reshape(1, 32), (P, 32)),
            "a_log": np.broadcast_to(np.asarray(ssd_a_log).reshape(1, 32), (P, 32))}
    packed = np.ascontiguousarray(np.concatenate([rows[n] for n, _ in VEC_SIZES], axis=1))

    i, j = np.arange(P)[:, None], np.arange(P)[None, :]
    q, k = np.arange(P)[:, None] % GRID_W, np.arange(GRID_W)[None, :]
    start = np.clip(q - WIN_C // 2, 0, GRID_W - WIN_C)
    mask = np.where((k >= start) & (k < start + WIN_C), 0.0, NEG)
    consts = np.concatenate([i == j, mask, i <= j, i >= j, i > j, i < j], axis=1).astype(np.float32)
    t, w = np.arange(LAT)[None, :], np.array(WINDOWS)[:, None]
    lo, hi = np.clip(t - w // 2, 0, LAT - 1), np.clip(t + w - 1 - w // 2, 0, LAT - 1)
    inverse = (1.0 / (hi - lo + 1)).astype(np.float32).reshape(1, -1)
    inverse = np.ascontiguousarray(np.broadcast_to(inverse, (P, inverse.shape[1])))

    arrays = {"in_x": x, "in_ctx": ctx, "in_vec": packed, "in_const": consts, "in_inv": inverse, "in_ada_w": ada_w,
              "in_w1": ffn_w1, "in_w3": ffn_w3, "in_w2": ffn_w2, "in_in_w": ssd_in_w, "in_pool_w": pool_w,
              "in_mix_w": mix_a_out_w, "in_qkv_w": na_qkv_w, "in_rpb": np.asarray(na_rpb)[..., ::-1], "in_na_w": na_out_w}
    arrays = {n: np.ascontiguousarray(a) for n, a in arrays.items()}
    nc = bacc.Bacc("TRN2", target_bir_lowering=False, num_devices=1)
    args = [nc.dram_tensor(n, a.shape, mybir.dt.from_np(a.dtype), kind="ExternalInput").ap()
            for n, a in arrays.items()]
    args.append(nc.dram_tensor("out_0", (1, LAT, D), F32, kind="ExternalOutput").ap())
    build(nc, *args)
    r = run_bass_kernel_spmd(nc, [arrays], core_ids=[0])
    return r.results[0]["out_0"]
```
